# Optimizing a Trainium2 kernel written in Bass

```python
import jax, jax.numpy as jnp
from jax import lax
import numpy as np

D_MODEL = 1024
BATCH = 1
SEQ = 1024
DEPTH = 1

GLA_HEADS = 4
GLA_V = D_MODEL // 2
GLA_DV = GLA_V // GLA_HEADS
GLA_DK = GLA_DV // 2
GLA_QK = GLA_HEADS * GLA_DK
GLA_GATE_RANK = 16
GLA_GATE_NORMALIZER = 16.0
HGRN_HEADS = 4
HGRN_V = D_MODEL - GLA_V
HGRN_DV = HGRN_V // HGRN_HEADS
HGRN_DK = 128
HGRN_K = HGRN_HEADS * HGRN_DK
MIX_WIDTH = GLA_V + HGRN_V
CHUNK = 64
D_FF = 4 * D_MODEL
N_MOD = 6
EPS = 1e-6

IN_SPLITS = (GLA_QK, GLA_QK, GLA_V, GLA_GATE_RANK, GLA_V,
             HGRN_K, HGRN_K, HGRN_V, HGRN_V)
IN_WIDTH = sum(IN_SPLITS)
IN_OFFSETS = [int(o) for o in np.cumsum(IN_SPLITS)[:-1]]

kernel_name = "hymba_style_gla_hgrn2_adaln_layer"

def rms_norm(x, gain=None):
    xf = x.astype(jnp.float32)
    y = xf * lax.rsqrt(jnp.mean(xf * xf, axis=-1, keepdims=True) + EPS)
    if gain is not None:
        y = y * gain.astype(jnp.float32)
    return y.astype(x.dtype)

def modulate(h, shift, scale):
    return h * (1.0 + scale[:, None, :]) + shift[:, None, :]

def split_heads(t, n_heads):
    b, s, w = t.shape
    return t.reshape(b, s, n_heads, w // n_heads).transpose(0, 2, 1, 3)

def merge_heads(t):
    b, h, s, d = t.shape
    return t.transpose(0, 2, 1, 3).reshape(b, s, h * d)

def chunk_gated_linear_attention(q, k, v, log_a, chunk):
    b, h, s, dk = q.shape
    dv = v.shape[-1]
    n = s // chunk
    q = q.reshape(b, h, n, chunk, dk)
    k = k.reshape(b, h, n, chunk, dk)
    v = v.reshape(b, h, n, chunk, dv)
    cum = jnp.cumsum(log_a.reshape(b, h, n, chunk, dk), axis=3)
    cum_mid = cum[:, :, :, chunk // 2 - 1:chunk // 2, :]
    cum_last = cum[:, :, :, chunk - 1:chunk, :]
    q_rel = q * jnp.exp(cum - cum_mid)
    k_rel = k * jnp.exp(cum_mid - cum)
    causal = jnp.tril(jnp.ones((chunk, chunk), dtype=bool))
    scores = jnp.where(causal, jnp.einsum('bhncd,bhnsd->bhncs', q_rel, k_rel), 0.0)
    o_intra = jnp.einsum('bhncs,bhnse->bhnce', scores, v)
    k_to_end = k * jnp.exp(cum_last - cum)
    chunk_update = jnp.einsum('bhncd,bhnce->bhnde', k_to_end, v)
    chunk_decay = jnp.exp(cum_last[:, :, :, 0, :])

    def step(state, inp):
        decay, update = inp
        return decay[..., None] * state + update, state

    state0 = jnp.zeros((b, h, dk, dv), dtype=q.dtype)
    _, states_prev = lax.scan(step, state0,
                              (jnp.moveaxis(chunk_decay, 2, 0), jnp.moveaxis(chunk_update, 2, 0)))
    states_prev = jnp.moveaxis(states_prev, 0, 2)
    o_inter = jnp.einsum('bhncd,bhnde->bhnce', q * jnp.exp(cum), states_prev)
    return (o_intra + o_inter).reshape(b, h, s, dv)

def hybrid_mixer(h, layer, w_in, gla_gate_w2, gla_gate_b2, gla_norm_g,
                 hgrn_lb_logits, hgrn_norm_g, w_out):
    f32 = jnp.float32
    proj = h @ w_in
    gq, gk, gv, g_lr, g_gate, hq, hf, hi, h_gate = jnp.split(proj, IN_OFFSETS, axis=-1)

    gate_logits = (g_lr @ gla_gate_w2 + gla_gate_b2).astype(f32)
    log_a_gla = jax.nn.log_sigmoid(gate_logits) / GLA_GATE_NORMALIZER
    o_gla = chunk_gated_linear_attention(
        split_heads(gq.astype(f32), GLA_HEADS) * (GLA_DK ** -0.5),
        split_heads(gk.astype(f32), GLA_HEADS),
        split_heads(gv.astype(f32), GLA_HEADS),
        split_heads(log_a_gla, GLA_HEADS), CHUNK)
    o_gla = merge_heads(rms_norm(o_gla, gla_norm_g)).astype(h.dtype) * jax.nn.silu(g_gate)

    lb = jnp.cumsum(jax.nn.softmax(hgrn_lb_logits.astype(f32), axis=0), axis=0)[layer]
    forget = lb + (1.0 - lb) * jax.nn.sigmoid(hf.astype(f32))
    o_hgrn = chunk_gated_linear_attention(
        split_heads(jax.nn.silu(hq.astype(f32)), HGRN_HEADS),
        split_heads(1.0 - forget, HGRN_HEADS),
        split_heads(hi.astype(f32), HGRN_HEADS),
        split_heads(jnp.log(forget), HGRN_HEADS), CHUNK)
    o_hgrn = merge_heads(rms_norm(o_hgrn, hgrn_norm_g)).astype(h.dtype) * jax.nn.silu(h_gate)

    return jnp.concatenate([o_gla, o_hgrn], axis=-1) @ w_out

def setup_inputs(seed: int = 0) -> dict:
    key = jax.random.key(seed)
    ks = jax.random.split(key, 14)
    nrm = jax.random.normal
    f32 = jnp.float32
    return {
        "x": nrm(ks[0], (BATCH, SEQ, D_MODEL), f32),
        "c": nrm(ks[1], (BATCH, D_MODEL), f32),
        "w_ada": nrm(ks[2], (DEPTH, D_MODEL, N_MOD * D_MODEL), f32) * (D_MODEL ** -0.5),
        "b_ada": nrm(ks[3], (DEPTH, N_MOD * D_MODEL), f32) * 0.02,
        "w_in": nrm(ks[4], (DEPTH, D_MODEL, IN_WIDTH), f32) * (D_MODEL ** -0.5),
        "gla_gate_w2": nrm(ks[5], (DEPTH, GLA_GATE_RANK, GLA_QK), f32) * (GLA_GATE_RANK ** -0.5),
        "gla_gate_b2": nrm(ks[6], (DEPTH, GLA_QK), f32) * 0.02,
        "gla_norm_g": 1.0 + 0.02 * nrm(ks[7], (DEPTH, GLA_DV), f32),
        "hgrn_lb_logits": nrm(ks[8], (DEPTH + 1, HGRN_K), f32) * 0.1,
        "hgrn_norm_g": 1.0 + 0.02 * nrm(ks[9], (DEPTH, HGRN_DV), f32),
        "w_out": nrm(ks[10], (DEPTH, MIX_WIDTH, D_MODEL), f32) * (MIX_WIDTH ** -0.5),
        "w_mlp1": nrm(ks[11], (DEPTH, D_MODEL, D_FF), f32) * (D_MODEL ** -0.5),
        "w_mlp2": nrm(ks[12], (DEPTH, D_FF, D_MODEL), f32) * (D_FF ** -0.5),
        "final_norm_g": 1.0 + 0.02 * nrm(ks[13], (D_MODEL,), f32),
    }

def reference(x, c, w_ada, b_ada, w_in, gla_gate_w2, gla_gate_b2, gla_norm_g,
              hgrn_lb_logits, hgrn_norm_g, w_out, w_mlp1, w_mlp2, final_norm_g):
    cond = jax.nn.silu(c)
    for layer in range(DEPTH):
        mod = cond @ w_ada[layer] + b_ada[layer]
        shift1, scale1, gate1, shift2, scale2, gate2 = jnp.split(mod, N_MOD, axis=-1)
        h = modulate(rms_norm(x), shift1, scale1)
        y = hybrid_mixer(h, layer, w_in[layer], gla_gate_w2[layer], gla_gate_b2[layer],
                         gla_norm_g[layer], hgrn_lb_logits, hgrn_norm_g[layer], w_out[layer])
        x = x + gate1[:, None, :] * y
        h = modulate(rms_norm(x), shift2, scale2)
        y = jnp.square(jax.nn.relu(h @ w_mlp1[layer])) @ w_mlp2[layer]
        x = x + gate2[:, None, :] * y
    return rms_norm(x, final_norm_g)


_drawn_inputs = setup_inputs


def setup_inputs(seed=0):
    import zlib

    import numpy as np

    out = dict(_drawn_inputs(seed))
    spreads = {}
    factors = {'gla_gate_b2': 8.0,
     'gla_norm_g': 8.0,
     'hgrn_lb_logits': 8.0,
     'hgrn_norm_g': 8.0,
     'final_norm_g': 2.838}
    for name, (base, spread) in spreads.items():
        noise = np.random.default_rng([zlib.crc32(name.encode()), seed]).standard_normal(out[name].shape)
        drawn = base * np.exp(spread * noise) if base else spread * noise
        out[name] = __import__('jax').numpy.asarray(drawn.astype(out[name].dtype))
    for name, factor in factors.items():
        out[name] = (out[name] * factor).astype(out[name].dtype)
    return out
```

```python
from contextlib import ExitStack

import concourse.bass as bass
from concourse import mybir

F32 = mybir.dt.float32
F32R = mybir.dt.float32r
U8 = mybir.dt.uint8
U32 = mybir.dt.uint32
ACT = mybir.ActivationFunctionType
ALU = mybir.AluOpType

P = 128
D = 1024
T = 1024
KT = D // P
HALF = T // 2
CH = 64
NC = T // CH
TT = T // P
DFF = 4 * D
EPS = 1e-6
NORMALIZER = 16.0
GQ, GK, GV, GLR, GG, HQ, HF, HI, HG = 0, 256, 512, 1024, 1040, 1552, 2064, 2576, 3088
RANK = 16
U_OUT = 29
U_MLP = 37
U_END = 101
BLOCKS = DFF // D
R_ADA, R_C, R_LB, R_GG, R_GH, R_B2, ROWS = 0, 48, 56, 64, 65, 66, 68


def attention_steps(own, prev):
    s = [[] for _ in range(8)]
    if own == "P":
        s[0] += [("z", 0, 0, 2), ("z", 0, 1, 3)]
    if prev == "P":
        s[0] += [("v", 1, 0, 0), ("k", 0, 0, 1)]
        s[1] += [("up", q, 0, q) for q in range(4)]
        s[2] += [("sc", 0, 0, 0), ("sc", 1, 0, 1), ("v", 1, 1, 2), ("k", 0, 1, 3)]
        s[3] += [("o", 0, 0, 2), ("o", 1, 0, 3), ("sc", 0, 1, 0), ("sc", 1, 1, 1)]
        s[4] += [("ss", 0, 0, 2), ("ss", 1, 0, 3), ("up", 4, 1, 0), ("up", 5, 1, 1)]
        s[5] += [("up", 6, 1, 2), ("up", 7, 1, 3)]
        s[6] += [("o", 0, 1, 0), ("o", 1, 1, 1)]
        s[7] += [("ss", 0, 1, 2), ("ss", 1, 1, 3)]
    if prev == "H":
        s[0] += [("k", 0, 0, 0)]
        s[1] += [("up", 0, 0, 2), ("up", 1, 0, 3), ("sc", 0, 0, 1)]
        s[2] += [("k", 0, 1, 0), ("sc", 0, 1, 1)]
        s[3] += [("o", 0, 0, 2)]
        s[4] += [("up", 2, 1, 3), ("up", 3, 1, 0), ("ss", 0, 0, 1)]
        s[5] += [("o", 0, 1, 2)]
        s[6] += [("ss", 0, 1, 3)]
    if own == "P" and prev is None:
        s[6] += [("ada", 1, 0, 2)]
    if own == "H" and prev == "P":
        s[5] += [("ada", 2, 0, 0)]
    if own in "PH":
        s[7] += [("v", 0, 0, 0), ("v", 0, 1, 1)]
    seen = {}
    for step in s:
        for n, piece in enumerate(step):
            step[n] = (*piece, seen.get(piece[0], 0))
            seen[piece[0]] = step[n][4] + 1
    return s


def before(kind, gi):
    if kind == "v":
        return (0, 2, 6)[gi] if isinstance(gi, int) and gi < 3 else 10 + 2 * (gi - 3)
    if kind == "k":
        return 0 if isinstance(gi, int) and gi < 1 else 2 * (gi - 1)
    if kind == "z":
        return 2 * gi
    if kind == "ada":
        return (1, 2, 2)[gi] if isinstance(gi, int) and gi < 3 else 3
    if kind == "up":
        return (0, 0, 8)[gi] if isinstance(gi, int) and gi < 3 else 16 + 4 * (gi - 3)
    if kind == "chunks":
        return (0, 0, 30)[gi] if isinstance(gi, int) and gi < 3 else 60 + 15 * (gi - 3)
    return (0, 0, 4)[gi] if isinstance(gi, int) and gi < 3 else 8 + 2 * (gi - 3)


def update_chunks(prev, q):
    per = 2 if prev == "P" else 4
    first = 2 * per * (q // 2) + q % 2
    return [n for n in range(first, first + 2 * per, 2) if n < NC - 1]


def chunks_after(prev, q):
    return min(8 * (q // 2 + 1), 30 if prev == "P" else 15)


GROUPS = {"P0": ("P", None), "P1": ("P", "P"), "H0": ("H", "P"), "H1": ("H", "H"), "G": ("G", "H")}
ADA_PLAN = {"P0": [2, 2, 2, 2, 2, 2, 0, 0], "P1": [0, 1, 1, 1, 1, 1, 1, 1], "H0": [3, 2, 2, 2, 0, 0, 0, 0]}


def hybrid_layer(nc, x, c, w_ada, b_ada, w_in, gate_w2, gate_b2, gla_g, lb_logits, hgrn_g, w_out, w1, w2,
                 final_g, out):
    steps = {name: attention_steps(*kinds) for name, kinds in GROUPS.items()}

    with ExitStack() as ctx:
        sem = lambda name: ctx.enter_context(nc.semaphore(name))
        bank = lambda name: ctx.enter_context(nc.psum_tensor(name, [P, HALF], F32))

        def at(name, kb, shape, dt=F32):
            return nc.alloc_sbuf_tensor_at(name, shape, dt, offset=int((17 + kb) * 1024))

        xT = at("xT", 0, [P, KT, T])
        a_hi = at("a_hi", 32, [P, KT, T], F32R)
        a_lo = at("a_lo", 64, [P, KT, T], F32R)
        a_full = at("a_full", 64, [P, KT, T])
        h_hi = at("h_hi", 96, [P, KT, T], F32R)
        h_lo = at("h_lo", 128, [P, KT, T], F32R)
        h_full = at("h_full", 128, [P, KT, T])
        out_stage = at("out_stage", 96, [P, TT, D])
        mixed = at("mixed", 96, [P, 8, T])
        ada_slots = [at(f"ada_slot{i}", kb, [P, D]) for i, kb in enumerate((96, 100, 104, 108, 152, 156, 120))]
        ada_acc = at("ada_acc", 112, [P, 2 * D])
        glr = at("glr", 120, [RANK, T])
        cum = at("cum", 124, [P, T])
        rows = at("rows", 124, [ROWS, P])
        k_end = at("k_end", 128, [P, T])
        k_rel = at("k_rel", 132, [P, T])
        q_rel = at("q_rel", 136, [P, T])
        q_cum = at("q_cum", 140, [P, T])
        x_stage = [at(f"x_stage{i}", 128 + 4 * i, [P, D]) for i in range(4)]
        v_nat = at("v_nat", 144, [P, 2, TT, P])
        masked = at("masked", 152, [P, 2, HALF])
        stat = at("stat", 156, [P, 2, HALF])
        raw = [at(f"raw{i}", 160 + 4 * i, [P, KT, P]) for i in range(2)]
        w_hi = [at(f"w_hi{i}", 168 + 4 * i, [P, KT, P], F32R) for i in range(2)]
        w_lo = [at(f"w_lo{i}", 176 + 4 * i, [P, KT, P], F32R) for i in range(2)]
        state = at("state", 184, [P, NC + 1, P])
        vT = [at(f"vT{i}", 184.5 + 4 * i, [P, T]) for i in range(2)]
        squares = at("squares", 184.5, [P, 4, HALF])
        k_nat = at("k_nat", 192.5, [P, 4, P])
        t0 = at("t0", 194.5, [P, T])
        t1 = at("t1", 198.5, [P, T])
        gain = at("gain", 194.5, [P, D])
        fin = at("fin", 198.5, [P, TT, 4])
        ones = at("ones", 202.5, [P, P])
        ident = at("ident", 203, [P, P])
        causal = at("causal", 203.5, [P, P])
        carry = at("carry", 204, [P, T], U8)
        w2s = at("w2s", 205, [RANK, 2 * P])
        mod = at("mod", 206, [P, 48])
        cols = at("cols", 206.1875, [P, ROWS])
        misc = at("misc", 206.46875, [P, 48])
        decay = at("decay", 206.6875, [P, NC])

        cond, cond_t = misc[:, 0:8], misc[:, 8:16]
        f_scale, f_bias = misc[:, 16:20], misc[:, 20:24]
        lb_m, lb_e, lb_s = misc[:, 24:28], misc[:, 28:36], misc[:, 36:40]
        eps, one = misc[:, 40:41], misc[:, 41:42]

        UB = [bank(f"unit_bank{i}") for i in range(4)]
        SB = [bank(f"small_bank{i}") for i in range(4)]

        rows_loaded, w2_loaded, gain_loaded = sem("rows_loaded"), sem("w2_loaded"), sem("gain_loaded")
        x_loaded = [sem(f"x_loaded{i}") for i in range(4)]
        ada_loaded = [sem(f"ada_loaded{i}") for i in range(7)]
        raw_loaded = [sem(f"raw_loaded{i}") for i in range(2)]
        consts, setup = sem("consts"), sem("setup")
        cond_ready, lb_exp = sem("cond_ready"), sem("lb_exp")
        squares1, sum1, squares2, sum2 = sem("squares1"), sem("sum1"), sem("squares2"), sem("sum2")
        rms_ready = sem("rms_ready")
        ada_added, scale_ready = sem("ada_added"), sem("scale_ready")
        normalised, modulated = sem("normalised"), sem("modulated")
        split_hi, lo_pool, lo_dve = sem("split_hi"), sem("lo_pool"), sem("lo_dve")
        whi_ready, wlo_ready = sem("whi_ready"), sem("wlo_ready")
        unit_filled, unit_read = sem("unit_filled"), sem("unit_read")
        filled = {k: sem(f"{k}_filled") for k in ("rows", "x", "stat", "ada", "z", "v", "k", "sc", "up", "o", "ss", "y")}
        read = {"rows": sem("cols_ready"), "x": sem("xT_ready"), "stat": sem("stat_ln"), "ada": sem("mod_ready"),
                "z": sem("z_min"), "v": sem("v_ready"), "k": sem("k_nat_ready"), "sc": sem("masked_ready"),
                "up": sem("state_ready"), "o": sem("o_copied"), "ss": sem("o_ln"), "y": sem("y_ready")}
        z_abs, z_exp, z_ln = sem("z_abs"), sem("z_exp"), sem("z_ln")
        forget_ready, hk_ready, q_silu = sem("forget_ready"), sem("hk_ready"), sem("q_silu")
        log_a, cum_ready, d_mid, d_last = sem("log_a"), sem("cum_ready"), sem("d_mid"), sem("d_last")
        e_q, e_k, e_end, e_cum = sem("e_q"), sem("e_k"), sem("e_end"), sem("e_cum")
        k_rel_ready, k_end_ready = sem("k_rel_ready"), sem("k_end_ready")
        q_rel_ready, q_cum_ready, decay_ready = sem("q_rel_ready"), sem("q_cum_ready"), sem("decay_ready")
        mask_zero = sem("mask_zero")
        o_squared, o_rms, normed = sem("o_squared"), sem("o_rms"), sem("normed")
        gate_silu, gated = sem("gate_silu"), sem("gated")
        hid_sq, hid_hi, hid_lo = sem("hid_sq"), sem("hid_hi"), sem("hid_lo")
        y_squared, y_sum, y_ln, y_rms = sem("y_squared"), sem("y_sum"), sem("y_ln"), sem("y_rms")
        stored = sem("stored")

        def tok(t, half):
            return t[:, half * HALF:(half + 1) * HALF]

        def row(t, k):
            return t[:, k] if isinstance(k, int) else t[:, bass.ds(k, 1)].rearrange("p a b -> p (a b)")

        def col(t, j):
            return t[:, j:j + 1] if isinstance(j, int) else t[:, bass.ds(j, 1)]

        def flat(t):
            return t.rearrange("p a b -> p (a b)")

        def chunked(t):
            return t[:, :].rearrange("p (n c) -> p n c", c=CH)

        def at_chunk(pos):
            return chunked(cum)[:, :, pos:pos + 1].broadcast_to([P, NC, CH])

        def reads(prev, p, gi):
            if p[0] == "up":
                return before("chunks", gi) + chunks_after(prev, p[1])
            return before(p[0], gi) + p[4] + 1

        def eight(e, body):
            for j in range(2):
                body(0, j)
            with e.Fori(1, 3) as i:
                for j in range(2):
                    body(i, j)
            for j in range(2):
                body(3, j)

        def step_is(i, j, i0, j0):
            return isinstance(i, int) and i == i0 and j == j0

        def mlp_blocks(e, body):
            with e.Fori(0, BLOCKS - 1) as b:
                body(b, False)
            body(BLOCKS - 1, True)

        def groups(e, group):
            group("P0", 0, None)
            group("P1", 1, None)
            group("H0", 2, 0)
            with e.Fori(1, 4) as h:
                group("H1", h + 2, h)
            group("G", 6, None)

        def y_bank(t, j):
            return (SB[0], SB[1], SB[2], SB[3], UB[0], UB[1], UB[2], UB[3])[2 * (t % 4) + j][:, :]

        def ada_slot(n):
            return (n % 6, max(n - 5, 0)) if n < 32 else (6, n if n > 32 else 0)

        def wait_ada(e, n):
            e.wait_ge(ada_loaded[ada_slot(n)[0]], 16 * (n // 6 + 1) if n < 32 else 16 * (n - 31))

        block = ctx.enter_context(nc.Block())

        @block.sync
        def _(sp):
            def load_x(t):
                if t >= 4:
                    sp.wait_ge(filled["x"], 2 * (t - 3))
                sp.dma_start(x_stage[t % 4][:, :], x[0, t * P:(t + 1) * P, :]).then_inc(x_loaded[t % 4], 16)

            def load_unit(u, slot, w, r, q):
                if not isinstance(u, int) or u >= 2:
                    sp.wait_ge(wlo_ready, u - 1)
                src = w[0, bass.ds(r, D), bass.ds(q, P)].rearrange("(k p) m -> p k m", p=P)
                sp.dma_start(raw[slot][:, :, :], src).then_inc(raw_loaded[slot], 16)

            def load_ada(n):
                slot, added = ada_slot(n)
                if added:
                    sp.wait_ge(ada_added, added)
                if n == 32:
                    sp.wait_ge(filled["z"], 4)
                g, q = divmod(n, 16)
                k, h = divmod(q, 2)
                sp.dma_start(ada_slots[slot][:, :], w_ada[0, k * P:(k + 1) * P, (2 * g + h) * D:(2 * g + h + 1) * D]
                             ).then_inc(ada_loaded[slot], 16)

            for src, r0, n in ((b_ada[0], R_ADA, 48), (c[0], R_C, 8), (lb_logits.rearrange("l n -> (l n)"), R_LB, 8),
                               (gla_g[0], R_GG, 1), (hgrn_g[0], R_GH, 1), (gate_b2[0], R_B2, 2)):
                sp.dma_start(rows[r0:r0 + n, :], src.rearrange("(r n) -> r n", n=P)).then_inc(rows_loaded, 16)
            sp.dma_start(w2s[:, :], gate_w2[0]).then_inc(w2_loaded, 16)
            for t in range(4):
                load_x(t)
            load_unit(0, 0, w_in, 0, GLR)
            for t in range(4, TT):
                load_x(t)
            for n in range(16):
                load_ada(n)
            load_unit(1, 1, w_in, 0, GK)
            for n in range(16, 20):
                load_ada(n)
            pair_cols = [GQ, GV, GV + P, GK + P, GQ + P, GV + 2 * P, GV + 3 * P]
            head_cols = [HF, HQ, HI, GG]
            n = 20
            for j, q in enumerate(pair_cols + head_cols):
                load_unit(2 + j, j % 2, w_in, 0, q)
                for _ in range(3 if n < 32 else 0 if j < 6 else 2 if j < 10 else 4):
                    load_ada(n)
                    n += 1
            while n < 48:
                load_ada(n)
                n += 1
            with sp.Fori(1, 4) as h:
                for j, q in enumerate(head_cols):
                    load_unit(4 * h + 9 + j, (1 + j) % 2, w_in, 0, h * P + q)
            for h in range(4):
                load_unit(25 + h, (1 + h) % 2, w_in, 0, HG + P * h)
            with sp.Fori(0, KT // 2) as i:
                for j in range(2):
                    load_unit(2 * i + U_OUT + j, (U_OUT + j) % 2, w_out, 0, i * (2 * P) + j * P)
            with sp.Fori(0, BLOCKS) as b:
                with sp.Fori(0, KT // 2) as i:
                    for j in range(2):
                        load_unit(16 * b + 2 * i + U_MLP + j, (U_MLP + j) % 2, w1, 0, b * D + i * (2 * P) + j * P)
                with sp.Fori(0, KT // 2) as i:
                    for j in range(2):
                        load_unit(16 * b + 2 * i + U_MLP + 8 + j, (U_MLP + j) % 2, w2, b * D, i * (2 * P) + j * P)
            sp.dma_start(gain[:, :], final_g.rearrange("(a n) -> a n", a=1).broadcast_to([P, D])
                         ).then_inc(gain_loaded, 16)
            for t in range(TT):
                sp.wait_ge(read["y"], 2 * (t + 1))
                sp.dma_start(out[0, t * P:(t + 1) * P, :], out_stage[:, t, :]).then_inc(stored, 16)
            sp.wait_ge(stored, 16 * TT)

        @block.gpsimd
        def _(pool):
            def low(u, slot):
                pool.wait_ge(whi_ready, u + 1)
                pool.tensor_tensor(w_lo[slot][:, :, :], raw[slot][:, :, :], w_hi[slot][:, :, :].bitcast(F32),
                                   ALU.subtract).then_inc(wlo_ready, 1)

            def split_low(n, full, hi, lo, half):
                for k in range(0, KT, 2):
                    pool.wait_ge(split_hi, n + half * KT + k + 1)
                    pool.tensor_tensor(tok(lo[:, k], half), tok(full[:, k], half), tok(hi[:, k], half).bitcast(F32),
                                       ALU.subtract).then_inc(lo_pool, 1)

            pool.memset(ones[:, :], 1.0).then_inc(consts, 1)
            pool.memset(ident[:, :], 0.0).then_inc(consts, 1)
            pool.memset(causal[:, :], 1.0).then_inc(consts, 1)
            pool.memset(carry[:, :], 1).then_inc(consts, 1)
            pool.wait_ge(consts, 4)
            pool.affine_select(out=ident[:, :], in_=ident[:, :], compare_op=ALU.not_equal, fill=1.0, base=0,
                               pattern=[[-1, P]], channel_multiplier=1).then_inc(consts, 1)
            pool.affine_select(out=causal[:, :], in_=causal[:, :], compare_op=ALU.is_ge, fill=0.0, base=0,
                               pattern=[[1, P]], channel_multiplier=-1).then_inc(consts, 1)
            pool.memset(chunked(carry)[:, :, 0:1], 0).then_inc(consts, 1)
            pool.wait_ge(consts, 7)
            pool.memset(causal[0:CH, CH:P], 0.0).then_inc(consts, 1)
            pool.memset(state[:, 0, :], 0.0).then_inc(consts, 1)
            pool.memset(eps, EPS).then_inc(consts, 1)
            pool.memset(one, 1.0).then_inc(consts, 1)
            pool.memset(t1[:, :], 0.0).then_inc(sum1, 1)
            for k in range(KT):
                pool.wait_ge(squares1, k + 1)
                pool.wait_ge(sum1, k + 1)
                pool.tensor_tensor(t1[:, :], t1[:, :], flat(squares[:, 2 * (k % 2):2 * (k % 2) + 2, :]),
                                   ALU.add).then_inc(sum1, 1)
            low(0, 0)
            low(1, 1)
            for half in range(2):
                split_low(0, a_full, a_hi, a_lo, half)
            for u in range(2, 13):
                low(u, u % 2)
            with pool.Fori(0, 4) as i:
                for j in range(4):
                    low(4 * i + 13 + j, (1 + j) % 2)
            low(29, 1)
            split_low(16, mixed, a_hi, a_lo, 0)
            low(30, 0)
            split_low(16, mixed, a_hi, a_lo, 1)
            pool.memset(t1[:, :], 0.0).then_inc(sum2, 1)

            def out_unit(i, j):
                for half in range(2):
                    n = 4 * i + 2 * j + half
                    pool.wait_ge(squares2, n + 1)
                    pool.wait_ge(sum2, n + 1)
                    pool.tensor_tensor(tok(t1, half), tok(t1, half), squares[:, 2 * j + half, :], ALU.add
                                       ).then_inc(sum2, 1)
                if not step_is(i, j, 3, 1):
                    low(2 * i + j + U_OUT + 2, (U_OUT + j) % 2)
            eight(pool, out_unit)
            split_low(32, h_full, h_hi, h_lo, 0)
            low(U_MLP + 1, (U_MLP + 1) % 2)
            split_low(32, h_full, h_hi, h_lo, 1)
            with pool.Fori(0, 31) as i:
                for j in range(2):
                    low(2 * i + U_MLP + 2 + j, (U_MLP + j) % 2)

        @block.scalar
        def _(act):
            def high(u, slot, loads):
                act.wait_ge(raw_loaded[slot], 16 * loads)
                if not isinstance(u, int) or u >= 2:
                    act.wait_ge(unit_filled, 2 * (u - 1))
                act.activation(w_hi[slot][:, :, :], raw[slot][:, :, :], ACT.Copy).then_inc(whi_ready, 1)

            def high_of(u):
                high(u, u % 2, u // 2 + 1)

            def split_high(full, hi, half, ready):
                for k in range(KT):
                    ready(half * KT + k, k)
                    act.activation(tok(hi[:, k], half), tok(full[:, k], half), ACT.Copy).then_inc(split_hi, 1)

            def inverse_rms(dst, n):
                for half in range(2):
                    act.wait_ge(filled["stat"], n + half + 1)
                    act.activation(tok(dst, half), SB[2 + half][:, :], ACT.Ln, bias=eps, scale=1.0 / D
                                   ).then_inc(read["stat"], 1)
                for half in range(2):
                    act.wait_ge(read["stat"], n + half + 1)
                    act.activation(tok(dst, half), tok(dst, half), ACT.Exp, scale=-0.5).then_inc(rms_ready, 1)

            act.wait_ge(read["rows"], 1)
            act.activation(cond_t, cols[:, R_C:R_C + 8], ACT.Tanh, scale=0.5).then_inc(cond_ready, 1)
            act.wait_ge(setup, 3)
            act.activation(lb_e, lb_e, ACT.Exp).then_inc(lb_exp, 1)
            high_of(0)
            act.wait_ge(consts, 11)
            for k in range(KT):
                act.wait_ge(read["x"], 15 if k < 4 else 16)
                if k >= 2:
                    act.wait_ge(sum1, k)
                act.activation(flat(squares[:, 2 * (k % 2):2 * (k % 2) + 2, :]), xT[:, k, :], ACT.Square
                               ).then_inc(squares1, 1)
            inverse_rms(t0, 0)
            high_of(1)
            for half in range(2):
                split_high(a_full, a_hi, half, lambda n, k: act.wait_ge(modulated, n + 1))
            for half in range(2):
                act.wait_ge(unit_filled, half + 1)
                act.activation(tok(glr, half), UB[half][0:RANK, :], ACT.Copy).then_inc(unit_read, 1)
            high_of(2)

            def group(name, gi, h):
                own, prev = GROUPS[name]
                s = steps[name]
                u0 = 4 * gi + 1

                def unit(j, half):
                    act.wait_ge(unit_filled, 2 * u0 + 2 * j + half + 1)
                    return UB[(2 + 2 * j + half) % 4][:, :]

                def next_high(j):
                    if name == "G" and j == 3:
                        return
                    high(u0 + j + 2, (1 + j) % 2, 2 * gi + (j + 3) // 2 + 1)

                def finished(kind):
                    total = sum(p[0] == kind for x in s for p in x)
                    if total:
                        act.wait_ge(filled[kind], before(kind, gi) + total)

                def copy_out(dst, j, func=ACT.Copy, **more):
                    for half in range(2):
                        act.activation(tok(dst, half), unit(j, half), func, **more).then_inc(unit_read, 1)

                def tanh_and_copy(j):
                    for half in range(2):
                        src = unit(j, half)
                        act.activation(tok(t0, half), src, ACT.Tanh, scale=0.5)
                        act.activation(tok(t1, half), src, ACT.Copy).then_inc(unit_read, 1)

                def read_out(slot):
                    for p in s[slot]:
                        kind, which, half, b, _ = p
                        if kind in ("up", "sc", "ada"):
                            continue
                        n = before(kind, gi) + p[4]
                        act.wait_ge(filled[kind], n + 1)
                        src = SB[b][:, :]
                        if kind == "z":
                            if gi > 0:
                                act.wait_ge(q_cum_ready, gi)
                            act.activation(tok(t0, half), src, ACT.Abs, bias=col(cols, R_B2 + gi)
                                           ).then_inc(z_abs, 1)
                        elif kind == "v":
                            act.activation(flat(v_nat[:, which, 4 * half:4 * half + 4, :]), src, ACT.Copy
                                           ).then_inc(read["v"], 1)
                        elif kind == "k":
                            act.activation(flat(k_nat[:, :, :]), src, ACT.Copy).then_inc(read["k"], 1)
                        elif kind == "o":
                            was = before("o", gi) + (half * (2 if prev == "P" else 1))
                            if not isinstance(was, int) or was > 0:
                                act.wait_ge(normed, was)
                            head = 2 * (gi - 1) + which if prev == "P" else gi + 1
                            act.activation(stat[:, which, :], src, ACT.Square).then_inc(o_squared, 1)
                            act.activation(tok(row(mixed, head), half), src, ACT.Copy).then_inc(read["o"], 1)
                        elif kind == "ss":
                            act.activation(stat[:, which, :], src, ACT.Ln, bias=eps, scale=1.0 / P
                                           ).then_inc(read["ss"], 1)
                            act.wait_ge(read["ss"], n + 1)
                            act.activation(stat[:, which, :], stat[:, which, :], ACT.Exp, scale=-0.5
                                           ).then_inc(o_rms, 1)

                if own == "G":
                    for slot in range(8):
                        read_out(slot)
                        if slot % 2:
                            j = slot // 2
                            act.wait_ge(gated, 4 + j)
                            tanh_and_copy(j)
                            next_high(j)
                    return

                sc = 1.0 / NORMALIZER if own == "P" else 1.0
                read_out(0)
                if own == "P":
                    if gi > 0:
                        act.wait_ge(k_end_ready, gi)
                    copy_out(t1, 0)
                    next_high(0)
                    act.wait_ge(z_abs, 2 * gi + 2)
                    act.activation(t0[:, :], t0[:, :], ACT.Exp, scale=-1.0).then_inc(z_exp, 1)
                    act.wait_ge(z_exp, gi + 1)
                    act.activation(t0[:, :], t0[:, :], ACT.Ln, bias=one).then_inc(z_ln, 1)
                    read_out(1)
                else:
                    if name == "H0":
                        act.wait_ge(q_cum_ready, 2)
                    else:
                        act.wait_ge(gated, h)
                    copy_out(t0, 0, ACT.Tanh, scale=0.5)
                    next_high(0)
                    read_out(1)
                    act.wait_ge(hk_ready, h + 1)
                    act.activation(t0[:, :], t0[:, :], ACT.Ln).then_inc(log_a, 1)
                read_out(2)
                read_out(3)
                next_high(1)
                finished("sc")
                act.wait_ge(d_mid, gi + 1)
                act.activation(q_rel[:, :], t0[:, :], ACT.Exp, scale=sc).then_inc(e_q, 1)
                act.activation(k_rel[:, :], t0[:, :], ACT.Exp, scale=-sc).then_inc(e_k, 1)
                finished("k")
                act.wait_ge(d_last, gi + 1)
                act.activation(k_end[:, :], t0[:, :], ACT.Exp, scale=-sc).then_inc(e_end, 1)
                if own == "P":
                    act.wait_ge(e_end, gi + 1)
                    copy_out(t0, 1)
                else:
                    act.wait_ge(k_end_ready, gi + 1)
                    tanh_and_copy(1)
                read_out(4)
                act.activation(cum[:, :], cum[:, :], ACT.Exp, scale=sc).then_inc(e_cum, 1)
                read_out(5)
                next_high(2)
                read_out(6)
                finished("o")
                copy_out(vT[0], 2)
                read_out(7)
                if own == "P":
                    copy_out(vT[1], 3)
                else:
                    act.wait_ge(q_cum_ready, gi + 1)
                    tanh_and_copy(3)
                next_high(3)

            groups(act, group)

            act.wait_ge(unit_filled, 2 * U_OUT)
            split_high(mixed, a_hi, 0, lambda n, k: act.wait_ge(gated, k + 1))
            high_of(30)
            split_high(mixed, a_hi, 1, lambda n, k: None)

            def high_of_pair(u, i, j):
                high(2 * i + u + j + 2, (u + j) % 2, i + ((u + j + 2) // 2 + 1))

            def out_unit(i, j):
                for half in range(2):
                    n = 4 * i + 2 * j + half
                    act.wait_ge(unit_read, n + 2 * U_OUT + 1)
                    if not (isinstance(i, int) and i == 0):
                        act.wait_ge(sum2, n - 2)
                    act.activation(squares[:, 2 * j + half, :], tok(row(xT, 2 * i + j), half), ACT.Square
                                   ).then_inc(squares2, 1)
                if not step_is(i, j, 3, 1):
                    high_of_pair(U_OUT, i, j)
            eight(act, out_unit)
            inverse_rms(t0, 2)
            split_high(h_full, h_hi, 0, lambda n, k: act.wait_ge(modulated, 16 + n + 1))
            high_of(U_MLP + 1)
            split_high(h_full, h_hi, 1, lambda n, k: act.wait_ge(modulated, 16 + n + 1))

            def mlp_block(b, last):
                def high_hidden(m, half, n):
                    act.wait_ge(hid_sq, 16 * b + n + 1)
                    act.activation(tok(row(a_hi, m), half), tok(row(a_full, m), half), ACT.Copy
                                   ).then_inc(hid_hi, 1)

                def up_unit(i, j):
                    for half in range(2):
                        n = 4 * i + 2 * j + half
                        g = 32 * b + n + 2 * U_MLP
                        first = step_is(i, j, 0, 0) and half == 0
                        if first:
                            act.wait_ge(unit_read, g)
                        act.wait_ge(unit_filled, g + 1)
                        act.activation(tok(row(a_full, 2 * i + j), half), UB[(2 * (U_MLP + j) + half) % 4][:, :],
                                       ACT.Relu).then_inc(unit_read, 1)
                        if not first:
                            high_hidden(2 * i + j - (1 - half), 1 - half, n - 1)
                    high_of_pair(U_MLP, 8 * b + i, j)
                eight(act, up_unit)
                high_hidden(KT - 1, 1, 15)

                def down_unit(i, j):
                    if not (last and isinstance(i, int) and i == 3):
                        high_of_pair(U_MLP + 8, 8 * b + i, j)
                eight(act, down_unit)
            mlp_blocks(act, mlp_block)

            for t in range(TT + 1):
                if t < TT:
                    for j in range(2):
                        if t >= 2:
                            act.wait_ge(y_squared, 2 * t + j - 3)
                        act.wait_ge(filled["y"], 2 * t + j + 1)
                        act.activation(squares[:, 2 * (t % 2) + j, :], y_bank(t, j), ACT.Square, accum_out=fin[:, t, j:j + 1]
                                       ).then_inc(y_squared, 1)
                if t > 0:
                    act.wait_ge(y_sum, t)
                    act.activation(fin[:, t - 1, 3:4], fin[:, t - 1, 2:3], ACT.Ln, bias=eps, scale=1.0 / D
                                   ).then_inc(y_ln, 1)
                    act.wait_ge(y_ln, t)
                    act.activation(fin[:, t - 1, 3:4], fin[:, t - 1, 3:4], ACT.Exp, scale=-0.5).then_inc(y_rms, 1)

        @block.tensor
        def _(pe):
            def product(out_ap, left, right, start=True, stop=True):
                return pe.matmul(out_ap, left, right, start=start, stop=stop)

            def unit(u, j, hi, lo, ready=None):
                for half in range(2):
                    dst = UB[(2 * j + half) % 4]
                    if not isinstance(u, int) or 2 * u + half > 3:
                        pe.wait_ge(unit_read, 2 * u + half - 3)
                    if half == 0:
                        pe.wait_ge(wlo_ready, u + 1)
                    for k in range(KT):
                        if ready:
                            ready(k, half)
                        wh, wl = w_hi[j % 2][:, k, :], w_lo[j % 2][:, k, :]
                        ah, al = tok(hi[:, k], half), tok(lo[:, k], half)
                        product(dst[:, :], wh, ah, k == 0, False)
                        product(dst[:, :], wh, al, False, False)
                        mm = product(dst[:, :], wl, ah, False, k == KT - 1)
                    mm.then_inc(unit_filled, 1)
                    yield half

            def split_ready(use):
                def ready(k, half):
                    pe.wait_ge(lo_dve if k % 2 else lo_pool, 8 * use + 4 * half + k // 2 + 1)
                return ready

            def turn(src, b):
                for i, tile in enumerate(src):
                    mm = pe.transpose(SB[b][:, i * P:(i + 1) * P], tile, ident[:, :])
                return mm

            def ada(g, b):
                pe.wait_ge(ada_added, 16 * (g + 1))
                for j in range(16):
                    mm = product(SB[b][:, j:j + 1], ada_acc[:, j * P:(j + 1) * P], ones[:, 0:1])
                mm.then_inc(filled["ada"], 1)

            def step(prev, p, gi, u0):
                kind, which, half, b, n = p
                mine = slice(CH * which, CH * which + CH) if prev == "P" else slice(0, P)
                width = 2 if prev == "P" else 1
                if kind == "ada":
                    return ada(which, b)
                if kind == "z":
                    pe.wait_ge(unit_read, 2)
                    pe.wait_ge(w2_loaded, 16)
                    mm = product(SB[b][:, :], w2s[:, gi * P:(gi + 1) * P], tok(glr, half))
                elif kind == "v":
                    if which == 0:
                        pe.wait_ge(unit_read, 2 * u0 + 4 + half + 1)
                    else:
                        pe.wait_ge(unit_read, 2 * u0)
                    mm = turn([vT[which][:, t * P:(t + 1) * P] for t in range(4 * half, 4 * half + 4)], b)
                elif kind == "k":
                    pe.wait_ge(k_end_ready, gi)
                    mm = turn([k_end[:, t * P:(t + 1) * P] for t in range(4 * half, 4 * half + 4)], b)
                elif kind == "sc":
                    pe.wait_ge(k_rel_ready, gi)
                    pe.wait_ge(q_rel_ready, gi)
                    for i in range(4):
                        t = slice((4 * half + i) * P, (4 * half + i + 1) * P)
                        mm = product(SB[b][:, i * P:(i + 1) * P], k_rel[mine, t], q_rel[mine, t])
                elif kind == "up":
                    pe.wait_ge(read["k"], before("k", gi) + half + 1)
                    pe.wait_ge(read["v"], before("v", gi) + (half + 1 if prev == "P" else 0))
                    for place, n in enumerate(update_chunks(prev, which)):
                        r = slice(CH * (n % 2), CH * (n % 2) + CH)
                        dst = SB[b][:, place * P * width:(place + 1) * P * width]
                        mm = product(dst, k_nat[r, (n // 2) % 4, :], v_nat[r, 0:width, n // 2, :])
                elif kind == "o":
                    at_n = (2 * half + which) if prev == "P" else half
                    pe.wait_ge(read["sc"], before("sc", gi) + at_n + 1)
                    pe.wait_ge(read["up"], before("chunks", gi) + (8 * half + 7) * width)
                    pe.wait_ge(q_cum_ready, gi)
                    slot = which if prev == "P" else half
                    for i in range(4):
                        t = 4 * half + i
                        product(SB[b][:, i * P:(i + 1) * P], v_nat[:, which, t, :], masked[:, slot, i * P:(i + 1) * P],
                                True, False)
                        for cc in range(2):
                            n = 2 * t + cc
                            mm = product(SB[b][:, i * P + cc * CH:i * P + cc * CH + CH], state[mine, n, :],
                                         q_cum[mine, n * CH:(n + 1) * CH], False, cc == 1)
                else:
                    pe.wait_ge(o_squared, before("o", gi) + n_of("ss", p) + 1)
                    mm = product(SB[b][:, :], ones[:, :], stat[:, which, :])
                mm.then_inc(filled[kind], 1)

            def n_of(kind, p):
                return p[4]

            pe.wait_ge(consts, 11)
            pe.wait_ge(rows_loaded, 16 * 6)
            pe.transpose(SB[2][:, 0:ROWS], rows[:, :], ident[0:ROWS, 0:ROWS]).then_inc(filled["rows"], 1)
            for t in range(TT):
                pe.wait_ge(x_loaded[t % 4], 16 * (t // 4 + 1))
                for j in range(2):
                    if t:
                        pe.wait_ge(read["x"], 2 * t + j - 1)
                    turn([x_stage[t % 4][:, (4 * j + i) * P:(4 * j + i + 1) * P] for i in range(4)], j
                         ).then_inc(filled["x"], 1)

            def feature_sums(n, sums, count):
                for half in range(2):
                    pe.wait_ge(sums, count(half))
                    product(SB[2 + half][:, :], ones[:, :], tok(t1, half)).then_inc(filled["stat"], 1)
            pe.wait_ge(read["rows"], 1)
            feature_sums(0, sum1, lambda half: 9)
            pe.wait_ge(read["stat"], 2)
            ada(0, 2)
            for _ in unit(0, 0, a_hi, a_lo, split_ready(0)):
                pass

            def group(name, gi, h):
                own, prev = GROUPS[name]
                u0 = 4 * gi + 1
                older = {"P0": [], "P1": ["P0"], "H0": ["P1"], "H1": ["H0", "H1"], "G": ["H1"]}[name]
                before_bank = [set() for _ in range(4)]
                for name_ in older:
                    for b in range(4):
                        before_bank[b] |= {[p for x in steps[name_] for p in x if p[3] == b][-1][0]}
                used = {}
                for jj in range(8):
                    j, half = divmod(jj, 2)
                    if half == 0:
                        halves = unit(u0 + j, 1 + j, a_hi, a_lo)
                    next(halves)
                    for p in steps[name][jj]:
                        b = p[3]
                        if b in used:
                            pe.wait_ge(read[used[b][0]], reads(prev, used[b], gi))
                        elif name == "P0":
                            kind, count = (("x", 16), ("x", 16), ("ada", 1), ("stat", 2))[b]
                            pe.wait_ge(read[kind], count)
                        else:
                            for kind in sorted(before_bank[b]):
                                pe.wait_ge(read[kind], before("chunks" if kind == "up" else kind, gi))
                        used[b] = p
                        step(prev, p, gi, u0)
                    if half == 1:
                        next(halves, None)

            groups(pe, group)

            def out_unit(i, j):
                for _ in unit(2 * i + U_OUT + j, U_OUT + j, a_hi, a_lo, split_ready(1) if step_is(i, j, 0, 0) else None):
                    pass
            eight(pe, out_unit)
            pe.wait_ge(read["o"], before("o", 7))
            pe.wait_ge(read["ss"], before("ss", 7))
            feature_sums(2, sum2, lambda half: 16 + half)

            def mlp_block(b, last):
                def up_unit(i, j):
                    for _ in unit(16 * b + 2 * i + U_MLP + j, U_MLP + j, h_hi, h_lo,
                                  split_ready(2) if step_is(i, j, 0, 0) else None):
                        pass

                def hidden_ready(k, half):
                    pe.wait_ge(hid_lo, 16 * b + 2 * k + half + 1)

                def down_unit(i, j):
                    for _ in unit(16 * b + 2 * i + U_MLP + 8 + j, U_MLP + j, a_hi, a_lo,
                                  hidden_ready if step_is(i, j, 0, 0) else None):
                        pass
                eight(pe, up_unit)
                eight(pe, down_unit)
            mlp_blocks(pe, mlp_block)

            pe.wait_ge(unit_read, 2 * U_END)
            for t in range(TT):
                for j in range(2):
                    if t >= 4:
                        pe.wait_ge(read["y"], 2 * (t - 4) + j + 1)
                    for i in range(4):
                        mm = pe.transpose(y_bank(t, j)[:, i * P:(i + 1) * P], xT[:, 4 * j + i, t * P:(t + 1) * P],
                                          ident[:, :])
                    mm.then_inc(filled["y"], 1)

        @block.vector
        def _(dve):
            def split_low(n, full, hi, lo, half, k):
                dve.wait_ge(split_hi, n + half * KT + k + 1)
                dve.tensor_tensor(tok(lo[:, k], half), tok(full[:, k], half), tok(hi[:, k], half).bitcast(F32),
                                  ALU.subtract).then_inc(lo_dve, 1)

            def add_ada(n):
                g, q = divmod(n, 16)
                k, h = divmod(q, 2)
                wait_ada(dve, n)
                src, acc = ada_slots[ada_slot(n)[0]][:, :], ada_acc[:, h * D:(h + 1) * D]
                if k == 0:
                    if g:
                        dve.wait_ge(filled["ada"], g)
                    dve.tensor_scalar(acc, src, col(cond, k), None, ALU.mult).then_inc(ada_added, 1)
                else:
                    dve.wait_ge(ada_added, n - 1)
                    dve.scalar_tensor_tensor(acc, src, col(cond, k), acc, ALU.mult, ALU.add).then_inc(ada_added, 1)

            def finish_ada(g):
                dve.wait_ge(filled["ada"], g + 1)
                dve.tensor_tensor(mod[:, 16 * g:16 * g + 16], SB[0 if g == 2 else 2][:, 0:16],
                                  cols[:, 16 * g:16 * g + 16], ALU.add).then_inc(read["ada"], 1)
                if g != 1:
                    at_ = 8 if g == 0 else 32
                    dve.wait_ge(read["ada"], g + 1)
                    dve.tensor_scalar(mod[:, at_:at_ + 8], mod[:, at_:at_ + 8], 1.0, None, ALU.add
                                      ).then_inc(scale_ready, 1)

            def modulate(n, full, hi, lo, shift, scale, norm):
                for half in range(2):
                    for k in range(KT + 1):
                        if k < KT:
                            norm(half, k)
                            dve.tensor_scalar(tok(full[:, k], half), tok(full[:, k], half), col(mod, scale + k),
                                              col(mod, shift + k), ALU.mult, ALU.add).then_inc(modulated, 1)
                        if k % 2 == 0 and k:
                            split_low(n, full, hi, lo, half, k - 1)

            chain = [0]

            def then(ins, wait=True):
                ins.then_inc(setup, 1)
                chain[0] += 1
                if wait:
                    dve.wait_ge(setup, chain[0])

            dve.wait_ge(filled["rows"], 1)
            dve.tensor_copy(cols[:, :], SB[2][:, 0:ROWS]).then_inc(read["rows"], 1)
            dve.wait_ge(read["rows"], 1)
            l0, l1 = cols[:, R_LB:R_LB + 4], cols[:, R_LB + 4:R_LB + 8]
            then(dve.tensor_tensor(lb_m, l0, l1, ALU.max))
            then(dve.tensor_tensor(lb_e[:, 0:4], l0, lb_m, ALU.subtract), False)
            then(dve.tensor_tensor(lb_e[:, 4:8], l1, lb_m, ALU.subtract))
            dve.wait_ge(cond_ready, 1)
            then(dve.scalar_tensor_tensor(cond, cond_t, 1.0, cols[:, R_C:R_C + 8], ALU.add, ALU.mult))
            then(dve.tensor_scalar(cond, cond, 0.5, None, ALU.mult))
            dve.wait_ge(lb_exp, 1)
            then(dve.tensor_tensor(lb_s, lb_e[:, 0:4], lb_e[:, 4:8], ALU.add))
            then(dve.reciprocal(lb_s, lb_s))
            then(dve.tensor_tensor(lb_m, lb_e[:, 0:4], lb_s, ALU.mult))
            then(dve.tensor_scalar(f_scale, lb_m, -0.5, 0.5, ALU.mult, ALU.add))
            then(dve.tensor_tensor(f_bias, lb_m, f_scale, ALU.add))
            for t in range(TT):
                for j in range(2):
                    dve.wait_ge(filled["x"], 2 * t + j + 1)
                    dve.tensor_copy(xT[:, 4 * j:4 * j + 4, t * P:(t + 1) * P],
                                    SB[j][:, :].rearrange("p (a b) -> p a b", a=4)).then_inc(read["x"], 1)
            for n in range(16):
                add_ada(n)
                if n >= 8:
                    k = n - 8
                    if k == 0:
                        dve.wait_ge(rms_ready, 2)
                        dve.wait_ge(read["x"], 16)
                    dve.tensor_tensor(a_full[:, k], xT[:, k], t0[:, :], ALU.mult).then_inc(normalised, 1)
            finish_ada(0)
            dve.wait_ge(scale_ready, 1)
            modulate(0, a_full, a_hi, a_lo, 0, 8, lambda half, k: dve.wait_ge(normalised, k + 1))
            for n in range(16, 20):
                add_ada(n)
            next_ada = [20]

            def group(name, gi, h):
                own, prev = GROUPS[name]
                s = steps[name]

                def finished(kind):
                    total = sum(p[0] == kind for x in s for p in x)
                    if total:
                        dve.wait_ge(filled[kind], before(kind, gi) + total)

                def read_out(slot):
                    for p in s[slot]:
                        kind, which, half, b, _ = p
                        if kind == "ada":
                            finish_ada(which)
                        if kind not in ("up", "sc", "ss", "z"):
                            continue
                        n = before(kind, gi) + p[4]
                        if kind == "z":
                            dve.wait_ge(z_abs, n + 1)
                            dve.tensor_scalar(tok(cum, half), SB[b][:, :], col(cols, R_B2 + gi), 0.0, ALU.add, ALU.min
                                              ).then_inc(read["z"], 1)
                        elif kind == "sc":
                            dve.wait_ge(filled["sc"], n + 1)
                            if name == "H1":
                                dve.memset(misc[:, 42 + half:43 + half], 0.0)
                            dve.wait_ge(consts, 11)
                            slot_ = which if prev == "P" else half
                            dve.copy_predicated(masked[:, slot_, :].rearrange("p (a b) -> p a b", a=4),
                                                causal[:, :].bitcast(U32)[:, None, :].broadcast_to([P, 4, P]),
                                                SB[b][:, :].rearrange("p (a b) -> p a b", a=4)
                                                ).then_inc(read["sc"], 1)
                        elif kind == "up":
                            dve.wait_ge(filled["up"], n + 1)
                            if which % 2 == 0:
                                even = b
                                continue
                            done = before("chunks", gi)
                            heads = 2 if prev == "P" else 1
                            both = [(nn, bb, place) for w, bb in ((which - 1, even), (which, b))
                                    for place, nn in enumerate(update_chunks(prev, w))]
                            for nn, bb, place in sorted(both):
                                for hd in range(heads):
                                    r = slice(CH * hd, CH * hd + CH) if prev == "P" else slice(0, P)
                                    at_ = (place * heads + hd) * P
                                    if nn:
                                        dve.wait_ge(read["up"], done + heads * (nn - 1) + hd + 1)
                                    dve.scalar_tensor_tensor(state[r, nn + 1, :], state[r, nn, :], decay[r, nn:nn + 1],
                                                             SB[bb][r, at_:at_ + P], ALU.mult, ALU.add
                                                             ).then_inc(read["up"], 1)
                        else:
                            dve.wait_ge(o_rms, n + 1)
                            head = 2 * (gi - 1) + which if prev == "P" else gi + 1
                            g = R_GG if prev == "P" else R_GH
                            dst = tok(row(mixed, head), half)
                            dve.scalar_tensor_tensor(dst, dst, cols[:, g:g + 1], stat[:, which, :], ALU.mult, ALU.mult
                                                     ).then_inc(normed, 1)
                    if name in ADA_PLAN:
                        for _ in range(ADA_PLAN[name][slot]):
                            add_ada(next_ada[0])
                            next_ada[0] += 1

                def gate(u, n, head):
                    dve.wait_ge(unit_read, 2 * u + 2)
                    dve.scalar_tensor_tensor(t0[:, :], t0[:, :], 1.0, t1[:, :], ALU.add, ALU.mult).then_inc(gate_silu, 1)
                    dve.wait_ge(gate_silu, n + 1)
                    if prev == "H" and own == "G":
                        dve.wait_ge(normed, before("ss", gi) + (2 if head == 7 else 0))
                    else:
                        dve.wait_ge(normed, before("ss", gi))
                    dst = row(mixed, head)
                    dve.scalar_tensor_tensor(dst, t0[:, :], 0.5, dst, ALU.mult, ALU.mult).then_inc(gated, 1)

                u0 = 4 * gi + 1
                if prev:
                    dve.wait_ge(decay_ready, gi)
                if own == "G":
                    for slot in range(8):
                        read_out(slot)
                        if slot % 2:
                            j = slot // 2
                            gate(u0 + j, 4 + j, 4 + j)
                    return
                read_out(0)
                if own == "P":
                    dve.wait_ge(z_ln, gi + 1)
                    dve.wait_ge(read["z"], 2 * gi + 2)
                    dve.scalar_tensor_tensor(t0[:, :], t0[:, :], -1.0, cum[:, :], ALU.mult, ALU.add
                                             ).then_inc(log_a, 1)
                else:
                    dve.wait_ge(unit_read, 2 * u0 + 2)
                    hh = h if h is not None else 0
                    dve.tensor_scalar(t0[:, :], t0[:, :], col(f_scale, hh), col(f_bias, hh), ALU.mult, ALU.add
                                      ).then_inc(forget_ready, 1)
                    dve.wait_ge(forget_ready, hh + 1)
                    dve.tensor_scalar(t1[:, :], t0[:, :], -1.0, 1.0, ALU.mult, ALU.add).then_inc(hk_ready, 1)
                read_out(1)
                dve.wait_ge(log_a, gi + 1)
                dve.tensor_tensor_scan(cum[:, :], carry[:, :], t0[:, :], 0.0, ALU.mult, ALU.add).then_inc(cum_ready, 1)
                dve.wait_ge(cum_ready, gi + 1)
                dve.tensor_tensor(chunked(t0), chunked(cum), at_chunk(CH // 2 - 1), ALU.subtract).then_inc(d_mid, 1)
                read_out(2)
                read_out(3)
                dve.wait_ge(e_k, gi + 1)
                dve.tensor_tensor(chunked(t0), chunked(cum), at_chunk(CH - 1), ALU.subtract).then_inc(d_last, 1)
                if own == "P":
                    dve.wait_ge(unit_read, 2 * u0 + 2)
                else:
                    dve.wait_ge(hk_ready, hh + 1)
                dve.tensor_tensor(k_rel[:, :], k_rel[:, :], t1[:, :], ALU.mult).then_inc(k_rel_ready, 1)
                dve.wait_ge(e_end, gi + 1)
                dve.tensor_tensor(k_end[:, :], k_end[:, :], t1[:, :], ALU.mult).then_inc(k_end_ready, 1)
                read_out(4)
                dve.wait_ge(unit_read, 2 * u0 + 4)
                if own == "H":
                    dve.scalar_tensor_tensor(t0[:, :], t0[:, :], 1.0, t1[:, :], ALU.add, ALU.mult).then_inc(q_silu, 1)
                    dve.wait_ge(q_silu, hh + 1)
                factor = float(CH) ** -0.5 if own == "P" else 0.5
                dve.wait_ge(e_q, gi + 1)
                dve.scalar_tensor_tensor(q_rel[:, :], t0[:, :], factor, q_rel[:, :], ALU.mult, ALU.mult
                                         ).then_inc(q_rel_ready, 1)
                read_out(5)
                read_out(6)
                if prev:
                    dve.wait_ge(read["up"], before("chunks", gi) + (30 if prev == "P" else 15))
                dve.wait_ge(e_cum, gi + 1)
                dve.tensor_copy(decay[:, :].rearrange("p (n c) -> p n c", c=1), chunked(cum)[:, :, CH - 1:CH]
                                ).then_inc(decay_ready, 1)
                finished("o")
                dve.scalar_tensor_tensor(q_cum[:, :], t0[:, :], factor, cum[:, :], ALU.mult, ALU.mult
                                         ).then_inc(q_cum_ready, 1)
                read_out(7)
                if name == "P0":
                    dve.memset(masked[:, :, :], 0.0).then_inc(mask_zero, 1)
                    dve.wait_ge(mask_zero, 1)
                if own == "H":
                    gate(u0 + 3, hh, hh)

            groups(dve, group)

            for half in range(2):
                for k in range(1, KT, 2):
                    split_low(16, mixed, a_hi, a_lo, half, k)

            def residual(u, u_ring, gate_col, m, first):
                for half in range(2):
                    if first and half == 0:
                        dve.wait_ge(unit_read, 2 * u)
                    dve.wait_ge(unit_filled, 2 * u + half + 1)
                    dst = tok(row(xT, m), half)
                    dve.scalar_tensor_tensor(dst, UB[(2 * u_ring + half) % 4][:, :], col(mod, gate_col + m), dst,
                                             ALU.mult, ALU.add).then_inc(unit_read, 1)

            dve.wait_ge(read["ada"], 3)
            eight(dve, lambda i, j: residual(2 * i + U_OUT + j, U_OUT + j, 16, 2 * i + j, step_is(i, j, 0, 0)))

            def norm2(half, k):
                if k == 0:
                    dve.wait_ge(rms_ready, 3 + half)
                    dve.wait_ge(unit_read, 2 * U_MLP)
                dve.tensor_tensor(tok(h_full[:, k], half), tok(xT[:, k], half), tok(t0, half), ALU.mult
                                  ).then_inc(normalised, 1)
                dve.wait_ge(normalised, KT + half * KT + k + 1)
            dve.wait_ge(scale_ready, 2)
            modulate(32, h_full, h_hi, h_lo, 24, 32, norm2)

            def mlp_block(b, last):
                def low_hidden(m, half, n):
                    dve.wait_ge(hid_hi, 16 * b + n + 1)
                    a = tok(row(a_hi, m), half).bitcast(F32)
                    dve.tensor_tensor(tok(row(a_lo, m), half), tok(row(a_full, m), half), a, ALU.subtract
                                      ).then_inc(hid_lo, 1)

                def up_unit(i, j):
                    for half in range(2):
                        n = 4 * i + 2 * j + half
                        dve.wait_ge(unit_read, 32 * b + n + 2 * U_MLP + 1)
                        t = tok(row(a_full, 2 * i + j), half)
                        dve.tensor_tensor(t, t, t, ALU.mult).then_inc(hid_sq, 1)
                        if not (step_is(i, j, 0, 0) and half == 0):
                            low_hidden(2 * i + j - (1 - half), 1 - half, n - 1)
                eight(dve, up_unit)
                low_hidden(KT - 1, 1, 15)
                eight(dve, lambda i, j: residual(16 * b + 2 * i + U_MLP + 8 + j, U_MLP + j, 40, 2 * i + j,
                                                 step_is(i, j, 0, 0)))
            mlp_blocks(dve, mlp_block)

            for t in range(TT + 1):
                if t < TT:
                    dve.wait_ge(y_squared, 2 * t + 2)
                    dve.tensor_tensor(fin[:, t, 2:3], fin[:, t, 0:1], fin[:, t, 1:2], ALU.add).then_inc(y_sum, 1)
                if t > 0:
                    dve.wait_ge(y_rms, t)
                    if t == 1:
                        dve.wait_ge(gain_loaded, 16)
                    for j in range(2):
                        cols_ = slice(j * HALF, (j + 1) * HALF)
                        dve.scalar_tensor_tensor(out_stage[:, t - 1, cols_], y_bank(t - 1, j), fin[:, t - 1, 3:4],
                                                 gain[:, cols_], ALU.mult, ALU.mult).then_inc(read["y"], 1)


_INS = ['x', 'c', 'w_ada', 'b_ada', 'w_in', 'gla_gate_w2', 'gla_gate_b2', 'gla_norm_g', 'hgrn_lb_logits',
        'hgrn_norm_g', 'w_out', 'w_mlp1', 'w_mlp2', 'final_norm_g']
_OUTS = [((1, T, D), 'float32')]


def kernel(**inputs):
    import numpy as _np
    import concourse.bacc as _bacc
    from concourse import mybir as _mybir
    from concourse.bass_utils import run_bass_kernel_spmd as _run

    nc = _bacc.Bacc("TRN2", target_bir_lowering=False, num_devices=1)
    arrays, args = {}, []
    for name in _INS:
        a = _np.ascontiguousarray(inputs[name])
        arrays[f"in_{name}_dram"] = a
        args.append(nc.dram_tensor(f"in_{name}_dram", a.shape, _mybir.dt.from_np(a.dtype), kind="ExternalInput").ap())
    for i, (shape, dtype) in enumerate(_OUTS):
        dt = _mybir.dt.from_np(_np.dtype(dtype))
        args.append(nc.dram_tensor(f"out_{i}_dram", shape, dt, kind="ExternalOutput").ap())
    hybrid_layer(nc, *args)
    r = _run(nc, [arrays], core_ids=[0])
    return r.results[0]["out_0_dram"]
```

```python
from contextlib import ExitStack

import concourse.bass as bass
from concourse import mybir

F32 = mybir.dt.float32
F32R = mybir.dt.float32r
U8 = mybir.dt.uint8
U32 = mybir.dt.uint32
ACT = mybir.ActivationFunctionType
ALU = mybir.AluOpType

P = 128
D = 1024
T = 1024
KT = D // P
HALF = T // 2
CH = 64
NC = T // CH
TT = T // P
DFF = 4 * D
EPS = 1e-6
NORMALIZER = 16.0
GQ, GK, GV, GLR, GG, HQ, HF, HI, HG = 0, 256, 512, 1024, 1040, 1552, 2064, 2576, 3088
RANK = 16
U_OUT = 29
U_MLP = 37
U_END = 101
BLOCKS = DFF // D
R_ADA, R_C, R_LB, R_GG, R_GH, R_B2, ROWS = 0, 48, 56, 64, 65, 66, 68


def attention_steps(own, prev):
    s = [[] for _ in range(8)]
    if own == "P":
        s[0] += [("z", 0, 0, 2), ("z", 0, 1, 3)]
    if prev == "P":
        s[0] += [("v", 1, 0, 0), ("k", 0, 0, 1)]
        s[1] += [("up", q, 0, q) for q in range(4)]
        s[2] += [("sc", 0, 0, 0), ("sc", 1, 0, 1), ("v", 1, 1, 2), ("k", 0, 1, 3)]
        s[3] += [("o", 0, 0, 2), ("o", 1, 0, 3), ("sc", 0, 1, 0), ("sc", 1, 1, 1)]
        s[4] += [("up", 4, 1, 0), ("up", 5, 1, 1), ("ss", 0, 0, 2), ("ss", 1, 0, 3)]
        s[5] += [("up", 6, 1, 2), ("up", 7, 1, 3)]
        s[6] += [("o", 0, 1, 0), ("o", 1, 1, 1)]
        s[7] += [("ss", 0, 1, 2), ("ss", 1, 1, 3)]
    if prev == "H":
        s[0] += [("k", 0, 0, 0)]
        s[1] += [("up", 0, 0, 2), ("up", 1, 0, 3), ("sc", 0, 0, 1)]
        s[2] += [("k", 0, 1, 0), ("sc", 0, 1, 1)]
        s[3] += [("o", 0, 0, 2)]
        s[4] += [("up", 2, 1, 3), ("up", 3, 1, 0), ("ss", 0, 0, 1)]
        s[5] += [("o", 0, 1, 2)]
        s[6] += [("ss", 0, 1, 3)]
    if own == "P" and prev is None:
        s[6] += [("ada", 1, 0, 2), ("ada", 1, 1, 3)]
        s[7] += [("ada", 1, 2, 2), ("ada", 1, 3, 3)]
    if own == "H" and prev == "P":
        s[5] += [("ada", 2, 0, 0), ("ada", 2, 1, 1)]
        s[6] += [("ada", 2, 2, 2), ("ada", 2, 3, 3)]
    if own in "PH":
        s[7] += [("v", 0, 0, 0), ("v", 0, 1, 1)]
    seen = {}
    for step in s:
        for n, piece in enumerate(step):
            step[n] = (*piece, seen.get(piece[0], 0))
            seen[piece[0]] = step[n][4] + 1
    return s


def before(kind, gi):
    if kind == "v":
        return (0, 2, 6)[gi] if isinstance(gi, int) and gi < 3 else 10 + 2 * (gi - 3)
    if kind == "k":
        return 0 if isinstance(gi, int) and gi < 1 else 2 * (gi - 1)
    if kind == "z":
        return 2 * gi
    if kind == "ada":
        return (4, 8, 8)[gi] if isinstance(gi, int) and gi < 3 else 12
    if kind == "split":
        return (0, 0, 2)[gi] if isinstance(gi, int) and gi < 3 else 4 + 2 * (gi - 3)
    if kind == "up":
        return (0, 0, 8)[gi] if isinstance(gi, int) and gi < 3 else 16 + 4 * (gi - 3)
    if kind == "chunks":
        return (0, 0, 30)[gi] if isinstance(gi, int) and gi < 3 else 60 + 15 * (gi - 3)
    return (0, 0, 4)[gi] if isinstance(gi, int) and gi < 3 else 8 + 2 * (gi - 3)


def update_chunks(prev, q):
    per = 2 if prev == "P" else 4
    first = 2 * per * (q // 2) + q % 2
    return [n for n in range(first, first + 2 * per, 2) if n < NC - 1]


def split_number(prev, which, half):
    return half if prev == "H" else which if half == 1 else None


def chunks_after(prev, q):
    return min(8 * (q // 2 + 1), 30 if prev == "P" else 15)


IN_TURN = ((0, 0), (0, 1), (1, 0), (1, 1))
BY_HALVES = ((0, 0), (1, 0), (0, 1), (1, 1))

GROUPS = {"P0": ("P", None), "P1": ("P", "P"), "H0": ("H", "P"), "H1": ("H", "H"), "G": ("G", "H")}
ADA_PLAN = {"P0": [2, 2, 2, 2, 2, 2, 0, 0], "P1": [0, 2, 2, 2, 0, 2, 3, 3], "H0": [1, 1, 0, 0, 0, 0, 0, 0]}
ADA_SLOT = [n % 6 if n < 32 else (2, 3, 6)[(n - 32) % 3] for n in range(48)]


def hybrid_layer(nc, x, c, w_ada, b_ada, w_in, gate_w2, gate_b2, gla_g, lb_logits, hgrn_g, w_out, w1, w2,
                 final_g, out):
    steps = {name: attention_steps(*kinds) for name, kinds in GROUPS.items()}

    with ExitStack() as ctx:
        sem = lambda name: ctx.enter_context(nc.semaphore(name))
        bank = lambda name: ctx.enter_context(nc.psum_tensor(name, [P, HALF], F32))

        def at(name, kb, shape, dt=F32):
            return nc.alloc_sbuf_tensor_at(name, shape, dt, offset=int((17 + kb) * 1024))

        xT = at("xT", 0, [P, KT, T])
        a_hi = at("a_hi", 32, [P, KT, T], F32R)
        a_lo = at("a_lo", 64, [P, KT, T], F32R)
        a_full = at("a_full", 64, [P, KT, T])
        h_hi = at("h_hi", 96, [P, KT, T], F32R)
        h_lo = at("h_lo", 128, [P, KT, T], F32R)
        h_full = at("h_full", 128, [P, KT, T])
        out_stage = at("out_stage", 96, [P, TT, D])
        mixed = at("mixed", 96, [P, 8, T])
        ada_slots = [at(f"ada_slot{i}", kb, [P, D]) for i, kb in enumerate((96, 100, 104, 108, 152, 156, 120))]
        ada_acc = at("ada_acc", 112, [P, 2 * D])
        glr = at("glr", 120, [RANK, T])
        cum = at("cum", 124, [P, T])
        rows = at("rows", 124, [ROWS, P])
        k_end = at("k_end", 128, [P, T])
        k_rel = at("k_rel", 132, [P, T])
        q_rel = at("q_rel", 136, [P, T])
        q_cum = at("q_cum", 140, [P, T])
        x_stage = [at(f"x_stage{i}", 128 + 4 * i, [P, D]) for i in range(4)]
        v_nat = at("v_nat", 144, [P, 2, TT, P])
        masked = at("masked", 152, [P, 2, HALF])
        stat = at("stat", 156, [P, 2, HALF])
        sq_lo = at("sq_lo", 156, [P, 2, HALF], F32R)
        sq_hi = at("sq_hi", 148, [P, 2, HALF], F32R)
        raw = [at(f"raw{i}", 160 + 4 * i, [P, KT, P]) for i in range(2)]
        w_hi = [at(f"w_hi{i}", 168 + 4 * i, [P, KT, P], F32R) for i in range(2)]
        w_lo = [at(f"w_lo{i}", 176 + 4 * i, [P, KT, P], F32R) for i in range(2)]
        state = at("state", 184, [P, NC + 1, P])
        vT = [at(f"vT{i}", 184.5 + 4 * i, [P, T]) for i in range(2)]
        squares = at("squares", 184.5, [P, 4, HALF])
        k_nat = at("k_nat", 192.5, [P, 4, P])
        t0 = at("t0", 194.5, [P, T])
        t1 = at("t1", 198.5, [P, T])
        gain = at("gain", 194.5, [P, D])
        fin = at("fin", 198.5, [P, TT, 4])
        ones_r = at("ones", 202.5, [P, P], F32R)
        ones = ones_r[:, :].bitcast(F32)
        ident = at("ident", 203, [P, P])
        causal = at("causal", 203.5, [P, P])
        carry = at("carry", 204, [P, T], U8)
        w2s = at("w2s", 205, [RANK, 2 * P])
        mod = at("mod", 206, [P, 48])
        cols = at("cols", 206.1875, [P, ROWS])
        misc = at("misc", 206.46875, [P, 48])
        decay = at("decay", 206.6875, [P, NC])
        x_stat = at("x_stat", 206.6875, [P, TT])

        cond, cond_t = misc[:, 0:8], misc[:, 8:16]
        f_scale, f_bias = misc[:, 16:20], misc[:, 20:24]
        lb_m, lb_e, lb_s = misc[:, 24:28], misc[:, 28:36], misc[:, 36:40]
        eps, one = misc[:, 40:41], misc[:, 41:42]

        UB = [bank(f"unit_bank{i}") for i in range(4)]
        SB = [bank(f"small_bank{i}") for i in range(4)]

        rows_loaded, w2_loaded, gain_loaded = sem("rows_loaded"), sem("w2_loaded"), sem("gain_loaded")
        x_loaded = [sem(f"x_loaded{i}") for i in range(4)]
        ada_loaded = [sem(f"ada_loaded{i}") for i in range(7)]
        raw_loaded = [sem(f"raw_loaded{i}") for i in range(2)]
        consts, setup = sem("consts"), sem("setup")
        cond_ready, lb_exp = sem("cond_ready"), sem("lb_exp")
        x_squared, x_rms, x_inverse, diag_ready = sem("x_squared"), sem("x_rms"), sem("x_inverse"), sem("diag_ready")
        squares2, sum2, rms_ready = sem("squares2"), sem("sum2"), sem("rms_ready")
        ada_added, ada_sum = sem("ada_added"), sem("ada_sum")
        normalised, modulated = sem("normalised"), sem("modulated")
        modulated_late = sem("modulated_late")
        split_hi, lo_pool, lo_dve = sem("split_hi"), sem("lo_pool"), sem("lo_dve")
        whi_ready, wlo_ready = sem("whi_ready"), sem("wlo_ready")
        unit_filled = [sem(f"unit_filled{half}") for half in range(2)]
        unit_read = [sem(f"unit_read{half}") for half in range(2)]
        filled = {k: sem(f"{k}_filled") for k in ("rows", "x", "stat", "ada", "z", "v", "k", "sc", "up", "o", "ss", "y")}
        read = {"rows": sem("cols_ready"), "x": sem("xT_ready"), "stat": sem("stat_ln"), "ada": sem("mod_ready"),
                "z": sem("z_min"), "v": sem("v_ready"), "k": sem("k_nat_ready"), "sc": sem("masked_ready"),
                "up": sem("state_ready"), "o": sem("o_copied"), "ss": sem("o_ln"), "y": sem("y_ready")}
        z_abs, z_exp, z_ln = sem("z_abs"), sem("z_exp"), sem("z_ln")
        forget_ready, hk_ready, q_silu = sem("forget_ready"), sem("hk_ready"), sem("q_silu")
        log_a, cum_ready, d_mid, d_last = sem("log_a"), sem("cum_ready"), sem("d_mid"), sem("d_last")
        e_q, e_k, e_end, e_cum = sem("e_q"), sem("e_k"), sem("e_end"), sem("e_cum")
        k_rel_ready, k_end_ready = sem("k_rel_ready"), sem("k_end_ready")
        q_rel_ready, q_cum_ready, decay_ready = sem("q_rel_ready"), sem("q_cum_ready"), sem("decay_ready")
        mask_zero = sem("mask_zero")
        sq_hi_ready, sq_lo_ready = sem("sq_hi_ready"), sem("sq_lo_ready")
        o_squared, o_rms, normed = sem("o_squared"), sem("o_rms"), sem("normed")
        gate_silu, gated = sem("gate_silu"), sem("gated")
        hid_sq, hid_hi, hid_lo = sem("hid_sq"), sem("hid_hi"), sem("hid_lo")
        y_squared, y_sum, y_rms, y_inverse = sem("y_squared"), sem("y_sum"), sem("y_rms"), sem("y_inverse")
        stored = sem("stored")

        def tok(t, half):
            return t[:, half * HALF:(half + 1) * HALF]

        def row(t, k):
            return t[:, k] if isinstance(k, int) else t[:, bass.ds(k, 1)].rearrange("p a b -> p (a b)")

        def col(t, j):
            return t[:, j:j + 1] if isinstance(j, int) else t[:, bass.ds(j, 1)]

        def flat(t):
            return t.rearrange("p a b -> p (a b)")

        def chunked(t):
            return t[:, :].rearrange("p (n c) -> p n c", c=CH)

        def at_chunk(pos):
            return chunked(cum)[:, :, pos:pos + 1].broadcast_to([P, NC, CH])

        def reads(prev, p, gi):
            if p[0] == "up":
                return before("chunks", gi) + chunks_after(prev, p[1])
            return before(p[0], gi) + p[4] + 1

        def eight(e, pair, first=IN_TURN, last=IN_TURN):
            pair(0, first)
            with e.Fori(1, 3) as i:
                pair(i, IN_TURN)
            pair(3, last)

        def is_pair(i, i0):
            return isinstance(i, int) and i == i0

        def mlp_blocks(e, body):
            body(0, False)
            with e.Fori(1, BLOCKS - 1) as b:
                body(b, False)
            body(BLOCKS - 1, True)

        def groups(e, group):
            group("P0", 0, None)
            group("P1", 1, None)
            group("H0", 2, 0)
            with e.Fori(1, 4) as h:
                group("H1", h + 2, h)
            group("G", 6, None)

        def y_bank(t, j):
            return (SB[0], SB[1], SB[2], SB[3], UB[2], UB[3])[2 * (t % 3) + j][:, :]

        def ada_piece(n):
            g, q = divmod(n, 16)
            return (g, q % 8, q // 8) if g == 0 else (g, q // 2, q % 2)

        def wait_ada(e, n):
            slot = ADA_SLOT[n]
            e.wait_ge(ada_loaded[slot], 16 * ADA_SLOT[:n + 1].count(slot))

        block = ctx.enter_context(nc.Block())

        @block.sync
        def _(sp):
            def load_x(t):
                if t >= 4:
                    sp.wait_ge(filled["x"], 2 * (t - 3))
                    sp.wait_ge(x_squared, t - 3)
                sp.dma_start(x_stage[t % 4][:, :], x[0, t * P:(t + 1) * P, :]).then_inc(x_loaded[t % 4], 16)

            def load_unit(u, slot, w, r, q):
                if not isinstance(u, int) or u >= 2:
                    sp.wait_ge(wlo_ready, u - 1)
                src = w[0, bass.ds(r, D), bass.ds(q, P)].rearrange("(k p) m -> p k m", p=P)
                sp.dma_start(raw[slot][:, :, :], src).then_inc(raw_loaded[slot], 16)

            def load_ada(n):
                slot = ADA_SLOT[n]
                last = [m for m in range(n) if ADA_SLOT[m] == slot][-1:]
                if last:
                    sp.wait_ge(ada_added, last[0] + 1)
                if n == 34:
                    sp.wait_ge(filled["z"], 4)
                g, k, h = ada_piece(n)
                if g == 0:
                    src = w_ada[0, k * P:(k + 1) * P, 0:2 * D].rearrange("p (a n) -> p a n", a=2)
                    sp.dma_start(ada_slots[slot][:, :].rearrange("p (a n) -> p a n", a=2),
                                 src[:, :, h * (D // 2):(h + 1) * (D // 2)]).then_inc(ada_loaded[slot], 16)
                else:
                    sp.dma_start(ada_slots[slot][:, :], w_ada[0, k * P:(k + 1) * P, (2 * g + h) * D:(2 * g + h + 1) * D]
                                 ).then_inc(ada_loaded[slot], 16)

            for t in range(3):
                load_x(t)
            for src, r0, n in ((b_ada[0], R_ADA, 48), (c[0], R_C, 8), (lb_logits.rearrange("l n -> (l n)"), R_LB, 8),
                               (gla_g[0], R_GG, 1), (hgrn_g[0], R_GH, 1), (gate_b2[0], R_B2, 2)):
                sp.dma_start(rows[r0:r0 + n, :], src.rearrange("(r n) -> r n", n=P)).then_inc(rows_loaded, 16)
            sp.dma_start(w2s[:, :], gate_w2[0]).then_inc(w2_loaded, 16)
            for t in range(3, TT):
                load_x(t)
            load_unit(0, 0, w_in, 0, GLR)
            for n in range(4):
                load_ada(n)
            load_unit(1, 1, w_in, 0, GK)
            for n in range(4, 16):
                load_ada(n)
            for n in range(16, 20):
                load_ada(n)
            pair_cols = [GQ, GV, GV + P, GK + P, GQ + P, GV + 2 * P, GV + 3 * P]
            head_cols = [HF, HQ, HI, GG]
            n = 20
            for j, q in enumerate(pair_cols + head_cols):
                load_unit(2 + j, j % 2, w_in, 0, q)
                for _ in range((3, 3, 3, 3, 0, 0, 3, 4, 4, 4, 1)[j]):
                    load_ada(n)
                    n += 1
            with sp.Fori(1, 4) as h:
                for j, q in enumerate(head_cols):
                    load_unit(4 * h + 9 + j, (1 + j) % 2, w_in, 0, h * P + q)
            for h in range(4):
                load_unit(25 + h, (1 + h) % 2, w_in, 0, HG + P * h)
            with sp.Fori(0, KT // 2) as i:
                for j in range(2):
                    load_unit(2 * i + U_OUT + j, (U_OUT + j) % 2, w_out, 0, i * (2 * P) + j * P)
            with sp.Fori(0, BLOCKS) as b:
                with sp.Fori(0, KT // 2) as i:
                    for j in range(2):
                        load_unit(16 * b + 2 * i + U_MLP + j, (U_MLP + j) % 2, w1, 0, b * D + i * (2 * P) + j * P)
                with sp.Fori(0, KT // 2) as i:
                    for j in range(2):
                        load_unit(16 * b + 2 * i + U_MLP + 8 + j, (U_MLP + j) % 2, w2, b * D, i * (2 * P) + j * P)
            sp.dma_start(gain[:, :], final_g.rearrange("(a n) -> a n", a=1).broadcast_to([P, D])
                         ).then_inc(gain_loaded, 16)
            for t in range(TT - 1):
                sp.wait_ge(read["y"], 2 * (t + 1))
                sp.dma_start(out[0, t * P:(t + 1) * P, :], out_stage[:, t, :]).then_inc(stored, 16)
            for j in range(2):
                sp.wait_ge(read["y"], 2 * TT - 1 + j)
                sp.dma_start(out[0, D - P:D, j * HALF:(j + 1) * HALF],
                             out_stage[:, TT - 1, j * HALF:(j + 1) * HALF]).then_inc(stored, 16)
            sp.wait_ge(stored, 16 * (TT + 1))

        @block.gpsimd
        def _(pool):
            def low(u, slot):
                pool.wait_ge(whi_ready, u + 1)
                pool.tensor_tensor(w_lo[slot][:, :, :], raw[slot][:, :, :], w_hi[slot][:, :, :].bitcast(F32),
                                   ALU.subtract).then_inc(wlo_ready, 1)

            pool.memset(ones[:, :], 1.0).then_inc(consts, 1)
            pool.memset(ident[:, :], 0.0).then_inc(consts, 1)
            pool.memset(causal[:, :], 1.0).then_inc(consts, 1)
            pool.memset(carry[:, :], 1).then_inc(consts, 1)
            pool.wait_ge(consts, 4)
            pool.affine_select(out=ident[:, :], in_=ident[:, :], compare_op=ALU.not_equal, fill=1.0, base=0,
                               pattern=[[-1, P]], channel_multiplier=1).then_inc(consts, 1)
            pool.affine_select(out=causal[:, :], in_=causal[:, :], compare_op=ALU.is_ge, fill=0.0, base=0,
                               pattern=[[1, P]], channel_multiplier=-1).then_inc(consts, 1)
            pool.memset(chunked(carry)[:, :, 0:1], 0).then_inc(consts, 1)
            pool.wait_ge(consts, 7)
            pool.memset(causal[0:CH, CH:P], 0.0).then_inc(consts, 1)
            pool.memset(state[:, 0, :], 0.0).then_inc(consts, 1)
            pool.memset(eps, EPS).then_inc(consts, 1)
            pool.memset(one, 1.0).then_inc(consts, 1)
            low(0, 0)

            def low_tiles(n, full, hi, lo, half, tiles):
                for i, k in enumerate(tiles):
                    pool.wait_ge(split_hi, n + 2 * i + 1)
                    pool.tensor_tensor(tok(lo[:, k], half), tok(full[:, k], half), tok(hi[:, k], half).bitcast(F32),
                                       ALU.subtract).then_inc(lo_pool, 1)

            pool.wait_ge(rms_ready, 2)
            pool.wait_ge(read["x"], 16)
            for k in range(KT):
                if k == 4:
                    low(1, 1)
                    low_tiles(0, a_full, a_hi, a_lo, 0, (0, 2))
                if k == 5:
                    low_tiles(4, a_full, a_hi, a_lo, 1, (0, 2))
                pool.tensor_tensor(a_full[:, k], xT[:, k], t0[:, :], ALU.mult).then_inc(normalised, 1)
            for half in range(2):
                low_tiles(8 + 4 * half, a_full, a_hi, a_lo, half, (4, 6))
            for u in range(2, 13):
                low(u, u % 2)
            with pool.Fori(0, 4) as i:
                for j in range(4):
                    low(4 * i + 13 + j, (1 + j) % 2)
            evens = (0, 2, 4, 6)
            low_tiles(16, mixed, a_hi, a_lo, 0, evens)
            low(29, 1)
            low(30, 0)
            low_tiles(24, mixed, a_hi, a_lo, 1, evens)
            pool.wait_ge(gated, 10)
            pool.memset(t1[:, :], 0.0).then_inc(sum2, 1)

            def add_squares(i, idx, half):
                n = 4 * i + idx
                pool.wait_ge(squares2, n + 1)
                pool.wait_ge(sum2, n + 1)
                pool.tensor_tensor(tok(t1, half), tok(t1, half), squares[:, idx, :], ALU.add).then_inc(sum2, 1)

            def out_pair(i, order):
                for idx, (j, half) in enumerate(order):
                    if is_pair(i, 3) and idx == 3:
                        low_tiles(32, h_full, h_hi, h_lo, 0, (0, 2))
                    add_squares(i, idx, half)
                    if half == 1:
                        low(2 * i + j + U_OUT + 2, (U_OUT + j) % 2)
            eight(pool, out_pair, last=BY_HALVES)
            low_tiles(36, h_full, h_hi, h_lo, 0, (4, 6))
            low_tiles(40, h_full, h_hi, h_lo, 1, evens)
            with pool.Fori(0, 31) as i:
                for j in range(2):
                    low(2 * i + U_MLP + 2 + j, (U_MLP + j) % 2)

        @block.scalar
        def _(act):
            def high(u, slot, loads):
                act.wait_ge(raw_loaded[slot], 16 * loads)
                if not isinstance(u, int) or u >= 2:
                    act.wait_ge(unit_filled[1], u - 1)
                act.activation(w_hi[slot][:, :, :], raw[slot][:, :, :], ACT.Copy).then_inc(whi_ready, 1)

            def high_of(u):
                high(u, u % 2, u // 2 + 1)

            def high_tile(full, hi, half, k):
                act.activation(tok(hi[:, k], half), tok(full[:, k], half), ACT.Copy).then_inc(split_hi, 1)

            def ahead(j, func):
                act.activation(col(misc, j), one, func)

            def modulate(dst, k, half, shift, scale):
                act.activation(tok(dst[:, k], half), tok(dst[:, k], half), ACT.Identity, bias=col(mod, shift + k),
                               scale=col(mod, scale + k)).then_inc(modulated, 1)

            def modulate_mlp(half, tiles):
                for i in range(len(tiles) + 1):
                    if i < len(tiles) and tiles[i] % 2 == 0:
                        act.wait_ge(normalised, KT * (1 + half) + tiles[i] + 1)
                        modulate(h_full, tiles[i], half, 24, 32)
                    if i:
                        k = tiles[i - 1]
                        act.wait_ge(modulated_late if k % 2 else modulated, 8 + 4 * half + k // 2 + 1)
                        high_tile(h_full, h_hi, half, k)

            def square_x(t):
                act.wait_ge(x_loaded[t % 4], 16 * (t // 4 + 1))
                if t >= 2:
                    act.wait_ge(x_squared, t - 1)
                act.activation(flat(squares[:, 2 * (t % 2):2 * (t % 2) + 2, :]), x_stage[t % 4][:, :], ACT.Square,
                               accum_out=x_stat[:, t:t + 1]).then_inc(x_squared, 1)

            for t in range(2):
                square_x(t)
            act.wait_ge(read["rows"], 1)
            act.activation(cond_t, cols[:, R_C:R_C + 8], ACT.Tanh, scale=0.5).then_inc(cond_ready, 1)
            act.wait_ge(setup, 3)
            act.activation(lb_e, lb_e, ACT.Exp).then_inc(lb_exp, 1)
            act.wait_ge(consts, 11)
            ahead(44, ACT.Sqrt)
            for t in range(2, TT):
                square_x(t)
            act.wait_ge(x_squared, TT)
            act.activation(x_stat[:, :], x_stat[:, :], ACT.Sqrt, bias=eps, scale=1.0 / D).then_inc(x_rms, 1)
            high_of(0)
            for half in range(2):
                act.wait_ge(filled["stat"], half + 1)
                act.activation(tok(t0, half), SB[2 + half][:, :], ACT.Copy).then_inc(rms_ready, 1)
            high_of(1)
            act.wait_ge(read["ada"], 2)
            for half in range(2):
                for k in range(5):
                    if k < 4:
                        act.wait_ge(normalised, k + 1)
                        modulate(a_full, k, half, 0, 8)
                    if k:
                        act.wait_ge(modulated, 4 * half + k)
                        high_tile(a_full, a_hi, half, k - 1)
            for half in range(2):
                for k in range(4, KT):
                    act.wait_ge(modulated_late, 4 * half + k - 3)
                    high_tile(a_full, a_hi, half, k)
            for half in range(2):
                act.wait_ge(unit_filled[half], 1)
                act.activation(tok(glr, half), UB[half][0:RANK, :], ACT.Copy).then_inc(unit_read[half], 1)
            high_of(2)

            def group(name, gi, h):
                own, prev = GROUPS[name]
                s = steps[name]
                u0 = 4 * gi + 1

                def unit(j, half):
                    act.wait_ge(unit_filled[half], u0 + j + 1)
                    return UB[(2 + 2 * j + half) % 4][:, :]

                def next_high(j):
                    high(u0 + j + 2, (1 + j) % 2, 2 * gi + (j + 3) // 2 + 1)

                def finished(kind):
                    total = sum(p[0] == kind for x in s for p in x)
                    if total:
                        act.wait_ge(filled[kind], before(kind, gi) + total)

                def copy_out(dst, j, func=ACT.Copy, **more):
                    for half in range(2):
                        act.activation(tok(dst, half), unit(j, half), func, **more).then_inc(unit_read[half], 1)

                def tanh_and_copy(j):
                    for half in range(2):
                        src = unit(j, half)
                        act.activation(tok(t0, half), src, ACT.Tanh, scale=0.5)
                        act.activation(tok(t1, half), src, ACT.Copy).then_inc(unit_read[half], 1)

                def read_out(slot):
                    logs, splits = [], []
                    for p in s[slot]:
                        kind, which, half, b, _ = p
                        if kind in ("up", "sc", "ada"):
                            continue
                        n = before(kind, gi) + p[4]
                        act.wait_ge(filled[kind], n + 1)
                        src = SB[b][:, :]
                        if kind == "z":
                            if gi > 0:
                                act.wait_ge(q_cum_ready, gi)
                            act.activation(tok(t0, half), src, ACT.Abs, bias=col(cols, R_B2 + gi)
                                           ).then_inc(z_abs, 1)
                        elif kind == "v":
                            act.activation(flat(v_nat[:, which, 4 * half:4 * half + 4, :]), src, ACT.Copy
                                           ).then_inc(read["v"], 1)
                        elif kind == "k":
                            act.activation(flat(k_nat[:, :, :]), src, ACT.Copy).then_inc(read["k"], 1)
                        elif kind == "o":
                            was = before("o", gi) + (half * (2 if prev == "P" else 1))
                            if not isinstance(was, int) or was > 0:
                                act.wait_ge(normed, was)
                            head = 2 * (gi - 1) + which if prev == "P" else gi + 1
                            if name == "H0":
                                act.wait_ge(ada_added, 48)
                            act.activation(stat[:, which, :], src, ACT.Square).then_inc(o_squared, 1)
                            act.activation(tok(row(mixed, head), half), src, ACT.Copy).then_inc(read["o"], 1)
                            if split_number(prev, which, half) is not None:
                                splits.append((which, n))
                        elif kind == "ss":
                            act.activation(stat[:, which, :], src, ACT.Ln, bias=eps, scale=1.0 / P
                                           ).then_inc(read["ss"], 1)
                            logs.append((which, n))
                    if splits and prev == "P":
                        finished("o")
                    for which, n in splits:
                        act.wait_ge(o_squared, n + 1)
                        act.activation(sq_hi[:, which, :], stat[:, which, :], ACT.Copy).then_inc(sq_hi_ready, 1)
                    for which, n in logs:
                        act.wait_ge(read["ss"], n + 1)
                        act.activation(stat[:, which, :], stat[:, which, :], ACT.Exp, scale=-0.5).then_inc(o_rms, 1)

                if own == "G":
                    for j in range(2):
                        read_out(2 * j)
                        read_out(2 * j + 1)
                        act.wait_ge(gated, 4 + j)
                        tanh_and_copy(j)
                        next_high(j)
                    for idx, (j, half) in enumerate(BY_HALVES):
                        if idx != 2:
                            read_out(4 + idx)
                        act.wait_ge(gated, 6 if idx < 2 else 5 + idx)
                        src = unit(2 + j, half)
                        act.activation(tok(t0, idx % 2), src, ACT.Tanh, scale=0.5)
                        act.activation(tok(t1, idx % 2), src, ACT.Copy).then_inc(unit_read[half], 1)
                        if idx == 1:
                            for k in range(KT):
                                act.wait_ge(gated, 6 if k < 6 else k + 1)
                                high_tile(mixed, a_hi, 0, k)
                        if half == 1:
                            next_high(2 + j)
                        if idx == 2:
                            read_out(4 + idx)
                    for k in range(KT):
                        if k >= 6:
                            act.wait_ge(gated, k + 3)
                        high_tile(mixed, a_hi, 1, k)
                    return

                sc = 1.0 / NORMALIZER if own == "P" else 1.0
                read_out(0)
                if own == "P":
                    if gi > 0:
                        act.wait_ge(k_end_ready, gi)
                    copy_out(t1, 0)
                    next_high(0)
                    act.wait_ge(z_abs, 2 * gi + 2)
                    act.activation(t0[:, :], t0[:, :], ACT.Exp, scale=-1.0).then_inc(z_exp, 1)
                    act.wait_ge(z_exp, gi + 1)
                    act.activation(t0[:, :], t0[:, :], ACT.Ln, bias=one).then_inc(z_ln, 1)
                    read_out(1)
                else:
                    if name == "H0":
                        act.wait_ge(q_cum_ready, 2)
                    else:
                        act.wait_ge(gated, h)
                    copy_out(t0, 0, ACT.Tanh, scale=0.5)
                    next_high(0)
                    read_out(1)
                    act.wait_ge(hk_ready, h + 1)
                    act.activation(t0[:, :], t0[:, :], ACT.Ln).then_inc(log_a, 1)
                read_out(2)
                read_out(3)
                next_high(1)
                finished("sc")
                act.wait_ge(d_mid, gi + 1)
                act.activation(q_rel[:, :], t0[:, :], ACT.Exp, scale=sc).then_inc(e_q, 1)
                act.activation(k_rel[:, :], t0[:, :], ACT.Exp, scale=-sc).then_inc(e_k, 1)
                finished("k")
                act.wait_ge(d_last, gi + 1)
                act.activation(k_end[:, :], t0[:, :], ACT.Exp, scale=-sc).then_inc(e_end, 1)
                if own == "P":
                    act.wait_ge(e_end, gi + 1)
                    copy_out(t0, 1)
                else:
                    act.wait_ge(k_end_ready, gi + 1)
                    tanh_and_copy(1)
                read_out(4)
                act.activation(cum[:, :], cum[:, :], ACT.Exp, scale=sc).then_inc(e_cum, 1)
                read_out(5)
                next_high(2)
                read_out(6)
                finished("o")
                copy_out(vT[0], 2)
                read_out(7)
                if own == "P":
                    copy_out(vT[1], 3)
                else:
                    act.wait_ge(q_cum_ready, gi + 1)
                    tanh_and_copy(3)
                next_high(3)

            groups(act, group)

            def high_of_pair(u, i, j):
                high(2 * i + u + j + 2, (u + j) % 2, i + ((u + j + 2) // 2 + 1))

            def out_pair(i, order):
                for idx, (j, half) in enumerate(order):
                    if is_pair(i, 3) and idx == 3:
                        inverse_rms(0)
                        act.wait_ge(read["ada"], 12)
                        modulate_mlp(0, (0, 1, 2))
                    act.wait_ge(unit_read[half], 2 * i + j + U_OUT + 1)
                    if not is_pair(i, 0):
                        act.wait_ge(sum2, 4 * i + idx - 2)
                    act.activation(squares[:, idx, :], tok(row(xT, 2 * i + j), half), ACT.Square).then_inc(squares2, 1)
                    if half == 1:
                        high_of_pair(U_OUT, i, j)

            def inverse_rms(half):
                act.wait_ge(filled["stat"], 2 + half + 1)
                act.activation(tok(t0, half), SB[2 + half][:, :], ACT.Ln, bias=eps, scale=1.0 / D
                               ).then_inc(read["stat"], 1)
                act.wait_ge(read["stat"], half + 1)
                act.activation(tok(t0, half), tok(t0, half), ACT.Exp, scale=-0.5).then_inc(rms_ready, 1)

            ahead(45, ACT.Ln)
            eight(act, out_pair, last=BY_HALVES)
            modulate_mlp(0, (3, 4, 5, 6, 7))
            ahead(46, ACT.Ln)
            inverse_rms(1)
            modulate_mlp(1, tuple(range(KT)))

            def mlp_block(b, last):
                behind = []

                def high_hidden():
                    if behind:
                        m, half, n = behind.pop()
                        act.wait_ge(hid_sq, 16 * b + n + 1)
                        act.activation(tok(row(a_hi, m), half), tok(row(a_full, m), half), ACT.Copy
                                       ).then_inc(hid_hi, 1)

                def up_pair(i, order):
                    for idx, (j, half) in enumerate(order):
                        m = 2 * i + j
                        if is_pair(i, 0) and j == 0:
                            act.wait_ge(unit_read[half], 16 * b + U_MLP)
                        act.wait_ge(unit_filled[half], 16 * b + m + U_MLP + 1)
                        act.activation(tok(row(a_full, m), half), UB[(2 * (U_MLP + j) + half) % 4][:, :],
                                       ACT.Relu).then_inc(unit_read[half], 1)
                        if idx:
                            high_hidden()
                        elif not is_pair(i, 0):
                            behind[:] = [(m - 1, 1, 4 * i - 1)]
                            high_hidden()
                        behind[:] = [(m, half, 4 * i + idx)]
                        if half == 1:
                            high_of_pair(U_MLP, 8 * b + i, j)
                eight(act, up_pair, first=BY_HALVES)
                high_hidden()

                def down_pair(i, order):
                    for j in range(2):
                        if not (last and is_pair(i, 3)):
                            high_of_pair(U_MLP + 8, 8 * b + i, j)
                eight(act, down_pair)
            mlp_blocks(act, mlp_block)

            for t in range(TT + 1):
                if t < TT:
                    for j in range(2):
                        if t >= 2:
                            act.wait_ge(y_squared, 2 * t + j - 3)
                        act.wait_ge(filled["y"], 2 * t + j + 1)
                        act.activation(squares[:, 2 * (t % 2) + j, :], y_bank(t, j), ACT.Square, accum_out=fin[:, t, j:j + 1]
                                       ).then_inc(y_squared, 1)
                if t > 0:
                    act.wait_ge(y_sum, t)
                    act.activation(fin[:, t - 1, 3:4], fin[:, t - 1, 2:3], ACT.Sqrt, bias=eps, scale=1.0 / D
                                   ).then_inc(y_rms, 1)

        @block.tensor
        def _(pe):
            def product(out_ap, left, right, start=True, stop=True):
                return pe.matmul(out_ap, left, right, start=start, stop=stop)

            def half_unit(u, j, half, hi, lo, ready=None, tiles=range(KT)):
                dst = UB[(2 * j + half) % 4]
                if tiles[0] == 0:
                    if not isinstance(u, int) or u >= 2:
                        pe.wait_ge(unit_read[half], u - 1)
                    pe.wait_ge(wlo_ready, u + 1)
                for k in tiles:
                    if ready:
                        ready(k, half)
                    wh, wl = w_hi[j % 2][:, k, :], w_lo[j % 2][:, k, :]
                    ah, al = tok(hi[:, k], half), tok(lo[:, k], half)
                    product(dst[:, :], wh, ah, k == 0, False)
                    product(dst[:, :], wh, al, False, False)
                    mm = product(dst[:, :], wl, ah, False, k == KT - 1)
                if tiles[-1] == KT - 1:
                    mm.then_inc(unit_filled[half], 1)

            def split_ready(use):
                def ready(k, half):
                    if use == 0:
                        n = 4 * (k // 4) + 2 * half + (k % 4) // 2 + 1
                    else:
                        n = 8 * use + 4 * half + k // 2 + 1
                    pe.wait_ge(lo_dve if k % 2 else lo_pool, n)
                return ready

            def turn(src, b):
                for i, tile in enumerate(src):
                    mm = pe.transpose(SB[b][:, i * P:(i + 1) * P], tile, ident[:, :])
                return mm

            def ada(g, q, b):
                pe.wait_ge(ada_added, 8 * (q // 2 + 1) if g == 0 else 16 * (g + 1))
                turn([ada_acc[:, (4 * q + j) * P:(4 * q + j + 1) * P] for j in range(4)], b).then_inc(filled["ada"], 1)

            def step(prev, p, gi, u0):
                kind, which, half, b, n = p
                mine = slice(CH * which, CH * which + CH) if prev == "P" else slice(0, P)
                width = 2 if prev == "P" else 1
                if kind == "ada":
                    return ada(which, half, b)
                if kind == "z":
                    pe.wait_ge(unit_read[half], 1)
                    pe.wait_ge(w2_loaded, 16)
                    mm = product(SB[b][:, :], w2s[:, gi * P:(gi + 1) * P], tok(glr, half))
                elif kind == "v":
                    if which == 0:
                        pe.wait_ge(unit_read[half], u0 + 3)
                    else:
                        pe.wait_ge(unit_read[half], u0)
                    mm = turn([vT[which][:, t * P:(t + 1) * P] for t in range(4 * half, 4 * half + 4)], b)
                elif kind == "k":
                    pe.wait_ge(k_end_ready, gi)
                    mm = turn([k_end[:, t * P:(t + 1) * P] for t in range(4 * half, 4 * half + 4)], b)
                elif kind == "sc":
                    pe.wait_ge(k_rel_ready, gi)
                    pe.wait_ge(q_rel_ready, gi)
                    for i in range(4):
                        t = slice((4 * half + i) * P, (4 * half + i + 1) * P)
                        mm = product(SB[b][:, i * P:(i + 1) * P], k_rel[mine, t], q_rel[mine, t])
                elif kind == "up":
                    pe.wait_ge(read["k"], before("k", gi) + half + 1)
                    pe.wait_ge(read["v"], before("v", gi) + (half + 1 if prev == "P" else 0))
                    for place, n in enumerate(update_chunks(prev, which)):
                        r = slice(CH * (n % 2), CH * (n % 2) + CH)
                        dst = SB[b][:, place * P * width:(place + 1) * P * width]
                        mm = product(dst, k_nat[r, (n // 2) % 4, :], v_nat[r, 0:width, n // 2, :])
                elif kind == "o":
                    at_n = (2 * half + which) if prev == "P" else half
                    pe.wait_ge(read["sc"], before("sc", gi) + at_n + 1)
                    pe.wait_ge(read["up"], before("chunks", gi) + (8 * half + 7) * width)
                    pe.wait_ge(q_cum_ready, gi)
                    slot = which if prev == "P" else half
                    for i in range(4):
                        t = 4 * half + i
                        product(SB[b][:, i * P:(i + 1) * P], v_nat[:, which, t, :], masked[:, slot, i * P:(i + 1) * P],
                                True, False)
                        for cc in range(2):
                            n = 2 * t + cc
                            mm = product(SB[b][:, i * P + cc * CH:i * P + cc * CH + CH], state[mine, n, :],
                                         q_cum[mine, n * CH:(n + 1) * CH], False, cc == 1)
                else:
                    at_n = split_number(prev, which, half)
                    if at_n is None:
                        pe.wait_ge(o_squared, before("o", gi) + n + 1)
                        mm = product(SB[b][:, :], ones[:, :], stat[:, which, :])
                    else:
                        pe.wait_ge(sq_lo_ready, before("split", gi) + at_n + 1)
                        product(SB[b][:, :], ones_r[:, :], sq_hi[:, which, :], True, False)
                        mm = product(SB[b][:, :], ones_r[:, :], sq_lo[:, which, :], False, True)
                mm.then_inc(filled[kind], 1)

            pe.wait_ge(consts, 11)
            for t in range(TT):
                if t == 2:
                    pe.wait_ge(rows_loaded, 16 * 6)
                    pe.transpose(SB[2][:, 0:ROWS], rows[:, :], ident[0:ROWS, 0:ROWS]).then_inc(filled["rows"], 1)
                pe.wait_ge(x_loaded[t % 4], 16 * (t // 4 + 1))
                for j in range(2):
                    if t:
                        pe.wait_ge(read["x"], 2 * t + j - 1)
                    turn([x_stage[t % 4][:, (4 * j + i) * P:(4 * j + i + 1) * P] for i in range(4)], j
                         ).then_inc(filled["x"], 1)

            def token_sums(half):
                product(SB[2 + half][:, :], ones[:, :], tok(t1, half)).then_inc(filled["stat"], 1)

            pe.wait_ge(read["rows"], 1)
            pe.wait_ge(diag_ready, 1)
            for half in range(2):
                token_sums(half)
            pe.wait_ge(rms_ready, 2)
            for q in range(2):
                ada(0, q, 2 + q)
            for half in range(2):
                half_unit(0, 0, half, a_hi, a_lo, split_ready(0), range(4))
            pe.wait_ge(read["x"], 16)
            for q in range(2, 4):
                ada(0, q, q - 2)
            for half in range(2):
                half_unit(1, 1, half, a_hi, a_lo, split_ready(0), range(4))
            for u in range(2):
                for half in range(2):
                    half_unit(u, u, half, a_hi, a_lo, split_ready(0), range(4, KT))

            def group(name, gi, h):
                own, prev = GROUPS[name]
                u0 = 4 * gi + 1
                older = {"P0": [], "P1": ["P0"], "H0": ["P1"], "H1": ["H0", "H1"], "G": ["H1"]}[name]
                before_bank = [set() for _ in range(4)]
                for name_ in older:
                    for b in range(4):
                        before_bank[b] |= {[p for x in steps[name_] for p in x if p[3] == b][-1][0]}
                used = {}
                for jj in range(8):
                    j, half = divmod(jj, 2)
                    if name == "G" and jj >= 4:
                        j, half = BY_HALVES[jj - 4]
                        j += 2
                    if not (name == "P0" and j == 0):
                        half_unit(u0 + j, 1 + j, half, a_hi, a_lo)
                    for p in steps[name][jj]:
                        b = p[3]
                        if b in used:
                            pe.wait_ge(read[used[b][0]], reads(prev, used[b], gi))
                        elif name == "P0":
                            kind, count = (("ada", 3), ("ada", 4), ("ada", 1), ("ada", 2))[b]
                            pe.wait_ge(read[kind], count)
                        else:
                            for kind in sorted(before_bank[b]):
                                pe.wait_ge(read[kind], before("chunks" if kind == "up" else kind, gi))
                        used[b] = p
                        step(prev, p, gi, u0)

            groups(pe, group)

            def first_mlp_pair():
                for half in range(2):
                    for tiles in (range(4), range(4, KT)) if half == 0 else (range(KT),):
                        for j in range(2):
                            half_unit(U_MLP + j, U_MLP + j, half, h_hi, h_lo, split_ready(2) if j == 0 else None, tiles)
                        if half == 0 and tiles[0] == 0:
                            pe.wait_ge(sum2, 17)
                            token_sums(1)

            def out_pair(i, order):
                for idx, (j, half) in enumerate(order):
                    u = 2 * i + U_OUT + j
                    if is_pair(i, 3) and idx == 2:
                        half_unit(u, U_OUT + j, half, a_hi, a_lo, None, range(5))
                        pe.wait_ge(read["o"], before("o", 7))
                        pe.wait_ge(read["ss"], before("ss", 7))
                        pe.wait_ge(sum2, 4 * 3 + 3)
                        token_sums(0)
                        half_unit(u, U_OUT + j, half, a_hi, a_lo, None, range(5, KT))
                    else:
                        half_unit(u, U_OUT + j, half, a_hi, a_lo, split_ready(1) if is_pair(i, 0) and j == 0 else None)
            eight(pe, out_pair, first=BY_HALVES, last=BY_HALVES)

            def mlp_block(b, last):
                def up_pair(i, order):
                    if b_first and is_pair(i, 0):
                        return first_mlp_pair()
                    for idx, (j, half) in enumerate(order):
                        half_unit(16 * b + 2 * i + U_MLP + j, U_MLP + j, half, h_hi, h_lo)

                def hidden_ready(k, half):
                    pe.wait_ge(hid_lo, 16 * b + (2 * half + k if k < 2 else 2 * k + half) + 1)

                def down_pair(i, order):
                    for idx, (j, half) in enumerate(order):
                        u = 16 * b + 2 * i + U_MLP + 8 + j
                        if last and is_pair(i, 3) and idx == 3:
                            turn_back(0)
                            turn_back(1)
                            half_unit(u, U_MLP + j, half, a_hi, a_lo, None, range(4))
                            turn_back(2)
                            half_unit(u, U_MLP + j, half, a_hi, a_lo, None, range(4, 7))
                            turn_back(3)
                            half_unit(u, U_MLP + j, half, a_hi, a_lo, None, range(7, KT))
                        else:
                            half_unit(u, U_MLP + j, half, a_hi, a_lo, hidden_ready if is_pair(i, 0) and j == 0 else None)
                b_first = isinstance(b, int) and b == 0
                eight(pe, up_pair, first=BY_HALVES)
                eight(pe, down_pair, last=BY_HALVES if last else IN_TURN)

            def turn_back(t):
                pe.wait_ge(unit_read[t // 4], U_END)
                if t == 2:
                    pe.wait_ge(unit_read[1], U_END - 1)
                for j in range(2):
                    if t >= 3:
                        pe.wait_ge(read["y"], 2 * (t - 3) + j + 1)
                    for i in range(4):
                        mm = pe.transpose(y_bank(t, j)[:, i * P:(i + 1) * P], xT[:, 4 * j + i, t * P:(t + 1) * P],
                                          ident[:, :])
                    mm.then_inc(filled["y"], 1)

            mlp_blocks(pe, mlp_block)
            for t in range(4, TT):
                turn_back(t)

        @block.vector
        def _(dve):
            def split_low(n, full, hi, lo, half, k):
                dve.wait_ge(split_hi, n)
                dve.tensor_tensor(tok(lo[:, k], half), tok(full[:, k], half), tok(hi[:, k], half).bitcast(F32),
                                  ALU.subtract).then_inc(lo_dve, 1)

            def add_ada(n):
                g, k, h = ada_piece(n)
                wait_ada(dve, n)
                src, acc = ada_slots[ADA_SLOT[n]][:, :], ada_acc[:, h * D:(h + 1) * D]
                if k == 0:
                    if g:
                        dve.wait_ge(filled["ada"], 4 * g)
                    dve.tensor_scalar(acc, src, col(cond, k), None, ALU.mult).then_inc(ada_added, 1)
                else:
                    dve.wait_ge(ada_added, n if g == 0 else n - 1)
                    dve.scalar_tensor_tensor(acc, src, col(cond, k), acc, ALU.mult, ALU.add).then_inc(ada_added, 1)

            def finish_ada(g, q, b):
                n = 4 * g + q
                at_ = 8 * (q % 2) + 4 * (q // 2) if g == 0 else 16 * g + 4 * q
                dst = mod[:, at_:at_ + 4]
                dve.wait_ge(filled["ada"], n + 1)
                dve.tensor_reduce(dst, SB[b][:, :].rearrange("p (a n) -> p a n", a=4), mybir.AxisListType.X, ALU.add
                                  ).then_inc(ada_sum, 1)
                dve.wait_ge(ada_sum, n + 1)
                dve.scalar_tensor_tensor(dst, dst, 1.0 if at_ in (8, 12, 32, 36) else 0.0, cols[:, at_:at_ + 4],
                                         ALU.add, ALU.add).then_inc(read["ada"], 1)

            chain = [0]

            def then(ins, wait=True):
                ins.then_inc(setup, 1)
                chain[0] += 1
                if wait:
                    dve.wait_ge(setup, chain[0])

            def copy_x(t):
                for j in range(2):
                    dve.wait_ge(filled["x"], 2 * t + j + 1)
                    dve.tensor_copy(xT[:, 4 * j:4 * j + 4, t * P:(t + 1) * P],
                                    SB[j][:, :].rearrange("p (a b) -> p a b", a=4)).then_inc(read["x"], 1)

            for t in range(2):
                copy_x(t)
            dve.wait_ge(filled["rows"], 1)
            dve.tensor_copy(cols[:, :], SB[2][:, 0:ROWS]).then_inc(read["rows"], 1)
            dve.wait_ge(read["rows"], 1)
            l0, l1 = cols[:, R_LB:R_LB + 4], cols[:, R_LB + 4:R_LB + 8]
            then(dve.tensor_tensor(lb_m, l0, l1, ALU.max))
            then(dve.tensor_tensor(lb_e[:, 0:4], l0, lb_m, ALU.subtract), False)
            then(dve.tensor_tensor(lb_e[:, 4:8], l1, lb_m, ALU.subtract))
            dve.wait_ge(cond_ready, 1)
            then(dve.scalar_tensor_tensor(cond, cond_t, 1.0, cols[:, R_C:R_C + 8], ALU.add, ALU.mult))
            then(dve.tensor_scalar(cond, cond, 0.5, None, ALU.mult))
            dve.wait_ge(lb_exp, 1)
            then(dve.tensor_tensor(lb_s, lb_e[:, 0:4], lb_e[:, 4:8], ALU.add))
            then(dve.reciprocal(lb_s, lb_s))
            then(dve.tensor_tensor(lb_m, lb_e[:, 0:4], lb_s, ALU.mult))
            then(dve.tensor_scalar(f_scale, lb_m, -0.5, 0.5, ALU.mult, ALU.add))
            then(dve.tensor_tensor(f_bias, lb_m, f_scale, ALU.add))
            for t in range(2, TT):
                copy_x(t)
            dve.wait_ge(x_rms, 1)
            dve.reciprocal(x_stat[:, :], x_stat[:, :]).then_inc(x_inverse, 1)
            dve.wait_ge(x_inverse, 1)
            dve.wait_ge(consts, 11)
            dve.tensor_tensor(t1[:, :].rearrange("p (a n) -> p a n", a=TT), ident[:, :][:, None, :].broadcast_to([P, TT, P]),
                              x_stat[:, :].rearrange("p (a n) -> p a n", n=1).broadcast_to([P, TT, P]), ALU.mult
                              ).then_inc(diag_ready, 1)
            for n in range(16):
                add_ada(n)
                if n == 8:
                    finish_ada(0, 0, 2)
                    finish_ada(0, 1, 3)
                if 11 <= n < 15:
                    i = n - 11
                    split_low(2 * i + 2, a_full, a_hi, a_lo, i // 2, 1 + 2 * (i % 2))
            finish_ada(0, 2, 0)
            finish_ada(0, 3, 1)
            dve.wait_ge(rms_ready, 2)
            dve.wait_ge(read["ada"], 4)
            for half in range(2):
                for k in range(4, KT + 2):
                    if k < KT:
                        dve.wait_ge(normalised, k + 1)
                        dve.tensor_scalar(tok(a_full[:, k], half), tok(a_full[:, k], half), col(mod, 8 + k), col(mod, k),
                                          ALU.mult, ALU.add).then_inc(modulated_late, 1)
                    if k in (7, 9):
                        split_low(8 + 4 * half + k - 5, a_full, a_hi, a_lo, half, k - 2)
            for n in range(16, 20):
                add_ada(n)
            next_ada = [20]

            def group(name, gi, h):
                own, prev = GROUPS[name]
                s = steps[name]

                def finished(kind):
                    total = sum(p[0] == kind for x in s for p in x)
                    if total:
                        dve.wait_ge(filled[kind], before(kind, gi) + total)

                def read_out(slot):
                    for p in s[slot]:
                        kind, which, half, b, _ = p
                        if kind == "ada":
                            finish_ada(which, half, b)
                        if kind == "o":
                            at_n = split_number(prev, which, half)
                            if at_n is not None:
                                dve.wait_ge(sq_hi_ready, before("split", gi) + at_n + 1)
                                dve.tensor_tensor(sq_lo[:, which, :], stat[:, which, :],
                                                  sq_hi[:, which, :].bitcast(F32), ALU.subtract).then_inc(sq_lo_ready, 1)
                        if kind not in ("up", "sc", "ss", "z"):
                            continue
                        n = before(kind, gi) + p[4]
                        if kind == "z":
                            dve.wait_ge(z_abs, n + 1)
                            dve.tensor_scalar(tok(cum, half), SB[b][:, :], col(cols, R_B2 + gi), 0.0, ALU.add, ALU.min
                                              ).then_inc(read["z"], 1)
                        elif kind == "sc":
                            dve.wait_ge(filled["sc"], n + 1)
                            if name == "H1":
                                dve.memset(misc[:, 42 + half:43 + half], 0.0)
                            dve.wait_ge(consts, 11)
                            slot_ = which if prev == "P" else half
                            dve.copy_predicated(masked[:, slot_, :].rearrange("p (a b) -> p a b", a=4),
                                                causal[:, :].bitcast(U32)[:, None, :].broadcast_to([P, 4, P]),
                                                SB[b][:, :].rearrange("p (a b) -> p a b", a=4)
                                                ).then_inc(read["sc"], 1)
                        elif kind == "up":
                            dve.wait_ge(filled["up"], n + 1)
                            if which % 2 == 0:
                                even = b
                                continue
                            done = before("chunks", gi)
                            heads = 2 if prev == "P" else 1
                            both = [(nn, bb, place) for w, bb in ((which - 1, even), (which, b))
                                    for place, nn in enumerate(update_chunks(prev, w))]
                            for nn, bb, place in sorted(both):
                                for hd in range(heads):
                                    r = slice(CH * hd, CH * hd + CH) if prev == "P" else slice(0, P)
                                    at_ = (place * heads + hd) * P
                                    if nn:
                                        dve.wait_ge(read["up"], done + heads * (nn - 1) + hd + 1)
                                    dve.scalar_tensor_tensor(state[r, nn + 1, :], state[r, nn, :], decay[r, nn:nn + 1],
                                                             SB[bb][r, at_:at_ + P], ALU.mult, ALU.add
                                                             ).then_inc(read["up"], 1)
                        else:
                            dve.wait_ge(o_rms, n + 1)
                            head = 2 * (gi - 1) + which if prev == "P" else gi + 1
                            g = R_GG if prev == "P" else R_GH
                            dst = tok(row(mixed, head), half)
                            dve.scalar_tensor_tensor(dst, dst, cols[:, g:g + 1], stat[:, which, :], ALU.mult, ALU.mult
                                                     ).then_inc(normed, 1)
                    if name in ADA_PLAN:
                        for _ in range(ADA_PLAN[name][slot]):
                            add_ada(next_ada[0])
                            next_ada[0] += 1

                def both_read(u):
                    for half in range(2):
                        dve.wait_ge(unit_read[half], u + 1)

                def gate(u, n, head, half=None, place=None):
                    th, xx = (t0[:, :], t1[:, :]) if half is None else (tok(t0, place), tok(t1, place))
                    for hf in (0, 1) if half is None else (half,):
                        dve.wait_ge(unit_read[hf], u + 1)
                    dve.scalar_tensor_tensor(th, th, 1.0, xx, ALU.add, ALU.mult).then_inc(gate_silu, 1)
                    dve.wait_ge(gate_silu, n + 1)
                    dve.wait_ge(normed, before("ss", gi) + (half + 1 if half is not None and head == 7 else 0))
                    dst = row(mixed, head) if half is None else tok(row(mixed, head), half)
                    dve.scalar_tensor_tensor(dst, th, 0.5, dst, ALU.mult, ALU.mult).then_inc(gated, 1)

                u0 = 4 * gi + 1
                def low_mixed(half):
                    for k in range(1, KT, 2):
                        split_low(16 + half * KT + k + 1, mixed, a_hi, a_lo, half, k)

                if prev:
                    dve.wait_ge(decay_ready, gi)
                if own == "G":
                    for j in range(2):
                        read_out(2 * j)
                        read_out(2 * j + 1)
                        gate(u0 + j, 4 + j, 4 + j)
                    for idx, (j, half) in enumerate(BY_HALVES):
                        if idx == 2:
                            low_mixed(0)
                        read_out(4 + idx)
                        gate(u0 + 2 + j, 6 + idx, 6 + j, half, idx % 2)
                    low_mixed(1)
                    return
                read_out(0)
                if own == "P":
                    dve.wait_ge(z_ln, gi + 1)
                    dve.wait_ge(read["z"], 2 * gi + 2)
                    dve.scalar_tensor_tensor(t0[:, :], t0[:, :], -1.0, cum[:, :], ALU.mult, ALU.add
                                             ).then_inc(log_a, 1)
                else:
                    both_read(u0)
                    hh = h if h is not None else 0
                    dve.tensor_scalar(t0[:, :], t0[:, :], col(f_scale, hh), col(f_bias, hh), ALU.mult, ALU.add
                                      ).then_inc(forget_ready, 1)
                    dve.wait_ge(forget_ready, hh + 1)
                    dve.tensor_scalar(t1[:, :], t0[:, :], -1.0, 1.0, ALU.mult, ALU.add).then_inc(hk_ready, 1)
                read_out(1)
                dve.wait_ge(log_a, gi + 1)
                dve.tensor_tensor_scan(cum[:, :], carry[:, :], t0[:, :], 0.0, ALU.mult, ALU.add).then_inc(cum_ready, 1)
                dve.wait_ge(cum_ready, gi + 1)
                dve.tensor_tensor(chunked(t0), chunked(cum), at_chunk(CH // 2 - 1), ALU.subtract).then_inc(d_mid, 1)
                read_out(2)
                read_out(3)
                dve.wait_ge(e_k, gi + 1)
                dve.tensor_tensor(chunked(t0), chunked(cum), at_chunk(CH - 1), ALU.subtract).then_inc(d_last, 1)
                if own == "P":
                    both_read(u0)
                else:
                    dve.wait_ge(hk_ready, hh + 1)
                dve.tensor_tensor(k_rel[:, :], k_rel[:, :], t1[:, :], ALU.mult).then_inc(k_rel_ready, 1)
                dve.wait_ge(e_end, gi + 1)
                dve.tensor_tensor(k_end[:, :], k_end[:, :], t1[:, :], ALU.mult).then_inc(k_end_ready, 1)
                read_out(4)
                both_read(u0 + 1)
                if own == "H":
                    dve.scalar_tensor_tensor(t0[:, :], t0[:, :], 1.0, t1[:, :], ALU.add, ALU.mult).then_inc(q_silu, 1)
                    dve.wait_ge(q_silu, hh + 1)
                factor = float(CH) ** -0.5 if own == "P" else 0.5
                dve.wait_ge(e_q, gi + 1)
                dve.scalar_tensor_tensor(q_rel[:, :], t0[:, :], factor, q_rel[:, :], ALU.mult, ALU.mult
                                         ).then_inc(q_rel_ready, 1)
                read_out(5)
                read_out(6)
                if prev:
                    dve.wait_ge(read["up"], before("chunks", gi) + (30 if prev == "P" else 15))
                dve.wait_ge(e_cum, gi + 1)
                dve.tensor_copy(decay[:, :].rearrange("p (n c) -> p n c", c=1), chunked(cum)[:, :, CH - 1:CH]
                                ).then_inc(decay_ready, 1)
                finished("o")
                dve.scalar_tensor_tensor(q_cum[:, :], t0[:, :], factor, cum[:, :], ALU.mult, ALU.mult
                                         ).then_inc(q_cum_ready, 1)
                read_out(7)
                if name == "P0":
                    dve.memset(masked[:, :, :], 0.0).then_inc(mask_zero, 1)
                    dve.wait_ge(mask_zero, 1)
                if own == "H":
                    gate(u0 + 3, hh, hh)

            groups(dve, group)

            def residual(u, u_ring, gate_col, m, half, first):
                if first:
                    dve.wait_ge(unit_read[half], u)
                dve.wait_ge(unit_filled[half], u + 1)
                dst = tok(row(xT, m), half)
                dve.scalar_tensor_tensor(dst, UB[(2 * u_ring + half) % 4][:, :], col(mod, gate_col + m), dst,
                                         ALU.mult, ALU.add).then_inc(unit_read[half], 1)

            def normalise(half, tiles):
                dve.wait_ge(rms_ready, 3 + half)
                dve.wait_ge(unit_read[half], U_MLP)
                for k in tiles:
                    if k < KT:
                        dve.tensor_tensor(tok(h_full[:, k], half), tok(xT[:, k], half), tok(t0, half), ALU.mult
                                          ).then_inc(normalised, 1)
                        if k % 2:
                            dve.wait_ge(normalised, KT * (1 + half) + k + 1)
                            dve.tensor_scalar(tok(h_full[:, k], half), tok(h_full[:, k], half), col(mod, 32 + k),
                                              col(mod, 24 + k), ALU.mult, ALU.add).then_inc(modulated_late, 1)
                    if k >= 3 and k % 2:
                        split_low(32 + half * KT + k - 1, h_full, h_hi, h_lo, half, k - 2)

            def out_pair(i, order):
                for idx, (j, half) in enumerate(order):
                    if is_pair(i, 3) and idx == 3:
                        normalise(0, (0, 1, 2))
                    residual(2 * i + U_OUT + j, U_OUT + j, 16, 2 * i + j, half, is_pair(i, 0) and j == 0)

            dve.wait_ge(read["ada"], 12)
            eight(dve, out_pair, first=BY_HALVES, last=BY_HALVES)
            normalise(0, range(3, KT + 2))
            normalise(1, range(KT + 2))

            def mlp_block(b, last):
                behind = []

                def low_hidden():
                    if behind:
                        m, half, n = behind.pop()
                        dve.wait_ge(hid_hi, 16 * b + n + 1)
                        dve.tensor_tensor(tok(row(a_lo, m), half), tok(row(a_full, m), half),
                                          tok(row(a_hi, m), half).bitcast(F32), ALU.subtract).then_inc(hid_lo, 1)

                def up_pair(i, order):
                    for idx, (j, half) in enumerate(order):
                        m = 2 * i + j
                        dve.wait_ge(unit_read[half], 16 * b + m + U_MLP + 1)
                        t = tok(row(a_full, m), half)
                        dve.tensor_tensor(t, t, t, ALU.mult).then_inc(hid_sq, 1)
                        if idx == 0 and not is_pair(i, 0):
                            behind[:] = [(m - 1, 1, 4 * i - 1)]
                        low_hidden()
                        behind[:] = [(m, half, 4 * i + idx)]
                eight(dve, up_pair, first=BY_HALVES)
                low_hidden()

                def down_pair(i, order):
                    for idx, (j, half) in enumerate(order):
                        if last and is_pair(i, 3) and idx == 3:
                            last_norm(range(3))
                        residual(16 * b + 2 * i + U_MLP + 8 + j, U_MLP + j, 40, 2 * i + j, half, is_pair(i, 0) and j == 0)
                eight(dve, down_pair, last=BY_HALVES if last else IN_TURN)

            def last_norm(tiles):
                for t in tiles:
                    if t < TT:
                        dve.wait_ge(y_squared, 2 * t + 2)
                        dve.tensor_tensor(fin[:, t, 2:3], fin[:, t, 0:1], fin[:, t, 1:2], ALU.add).then_inc(y_sum, 1)
                    if t > 0:
                        dve.wait_ge(y_rms, t)
                        dve.reciprocal(fin[:, t - 1, 3:4], fin[:, t - 1, 3:4]).then_inc(y_inverse, 1)
                        dve.wait_ge(y_inverse, t)
                        if t == 1:
                            dve.wait_ge(gain_loaded, 16)
                        for j in range(2):
                            cols_ = slice(j * HALF, (j + 1) * HALF)
                            dve.scalar_tensor_tensor(out_stage[:, t - 1, cols_], y_bank(t - 1, j), fin[:, t - 1, 3:4],
                                                     gain[:, cols_], ALU.mult, ALU.mult).then_inc(read["y"], 1)

            mlp_blocks(dve, mlp_block)
            last_norm(range(3, TT + 1))


_INS = ['x', 'c', 'w_ada', 'b_ada', 'w_in', 'gla_gate_w2', 'gla_gate_b2', 'gla_norm_g', 'hgrn_lb_logits',
        'hgrn_norm_g', 'w_out', 'w_mlp1', 'w_mlp2', 'final_norm_g']
_OUTS = [((1, T, D), 'float32')]


def kernel(**inputs):
    import numpy as _np
    import concourse.bacc as _bacc
    from concourse import mybir as _mybir
    from concourse.bass_utils import run_bass_kernel_spmd as _run

    nc = _bacc.Bacc("TRN2", target_bir_lowering=False, num_devices=1)
    arrays, args = {}, []
    for name in _INS:
        a = _np.ascontiguousarray(inputs[name])
        arrays[f"in_{name}_dram"] = a
        args.append(nc.dram_tensor(f"in_{name}_dram", a.shape, _mybir.dt.from_np(a.dtype), kind="ExternalInput").ap())
    for i, (shape, dtype) in enumerate(_OUTS):
        dt = _mybir.dt.from_np(_np.dtype(dtype))
        args.append(nc.dram_tensor(f"out_{i}_dram", shape, dt, kind="ExternalOutput").ap())
    hybrid_layer(nc, *args)
    r = _run(nc, [arrays], core_ids=[0])
    return r.results[0]["out_0_dram"]
```
